# Optimizing a Trainium2 kernel written in Bass

```python
import math
import jax, jax.numpy as jnp
from jax import lax
import numpy as np

D_MODEL = 1024
BATCH = 1
SEQ = 128
DEPTH = 2
DEC_BATCH = 1
DEC_SEQ = 256
PAST_LEN = 128

GRID_W = 64
EPS = 1e-6
N_MOD = 6

POOL_GROUPS = 4
POOL_WINDOWS = (2, 4, 8, 16)
POOL_DIM = D_MODEL // 2
POOL_GROUP_DIM = POOL_DIM // POOL_GROUPS

ATT_HEADS = 4
ATT_QK_DIM = 64
ATT_V_DIM = 2 * ATT_QK_DIM
ATT_QK_TOTAL = ATT_HEADS * 2 * ATT_QK_DIM
ATT_DIM = ATT_HEADS * ATT_V_DIM
ROPE_BASE = 10000.0
Q_BLOCK = 128

SSD_DIM = D_MODEL // 2
SSD_HEAD_DIM = 64
SSD_HEADS = SSD_DIM // SSD_HEAD_DIM
SSD_GROUPS = 2
SSD_STATE = 128
SSD_CONV_W = 3
SSD_CHUNK = 128
SSD_XBC_DIM = SSD_DIM + 2 * SSD_GROUPS * SSD_STATE

MIX_DIM = POOL_DIM + ATT_DIM + SSD_DIM
IN_SIZES = (POOL_DIM, ATT_QK_TOTAL, ATT_QK_TOTAL, ATT_DIM, SSD_DIM, SSD_XBC_DIM, 2 * SSD_HEADS)
IN_DIM = sum(IN_SIZES)

FFN_DIM = ((8 * D_MODEL // 3 + 127) // 128) * 128
FFN_CONV_W = 3

kernel_name = 'hybrid_flow_prefix_trunk'

def split_sizes(x, sizes, axis=-1):
    idx, acc = [], 0
    for s in sizes[:-1]:
        acc += s
        idx.append(acc)
    return jnp.split(x, idx, axis=axis)

def rmsnorm(x, g):
    xf = x.astype(jnp.float32)
    y = xf * lax.rsqrt(jnp.mean(xf * xf, axis=-1, keepdims=True) + EPS)
    return (y * g.astype(jnp.float32)).astype(x.dtype)

def dwconv_centred(x, w, b):
    k = w.shape[0]
    y = lax.conv_general_dilated(x, w[:, None, :].astype(x.dtype), window_strides=(1,),
                                 padding=[(k // 2, k // 2)],
                                 dimension_numbers=('NWC', 'WIO', 'NWC'),
                                 feature_group_count=x.shape[-1])
    return y + b.astype(x.dtype)

def multiscale_pool_mixer(u, pool_w, pool_scale):
    b, n, _ = u.shape
    uf = u.astype(jnp.float32).reshape(b, n, POOL_GROUPS, POOL_GROUP_DIM)
    cs = jnp.concatenate([jnp.zeros_like(uf[:, :1]), jnp.cumsum(uf, axis=1)], axis=1)
    half = jnp.array([w // 2 for w in POOL_WINDOWS], jnp.int32)
    t = jnp.arange(n, dtype=jnp.int32)[:, None]
    lo = jnp.clip(t - half, 0, n - 1)
    hi = jnp.clip(t + half - 1, 0, n - 1)
    g = jnp.arange(POOL_GROUPS, dtype=jnp.int32)[None, :]
    win_sum = cs[:, hi + 1, g, :] - cs[:, lo, g, :]
    count = (hi - lo + 1).astype(jnp.float32)[None, :, :, None]
    pooled = (win_sum / count - uf).astype(u.dtype)
    mixed = jnp.einsum('blgd,gde->blge', pooled, pool_w) * pool_scale.reshape(POOL_GROUPS, POOL_GROUP_DIM)
    return mixed.reshape(b, n, POOL_DIM)

def axial_rope_angles(n_tokens):
    rows = n_tokens // GRID_W
    row = jnp.repeat(jnp.arange(rows), GRID_W).astype(jnp.float32)
    col = jnp.tile(jnp.arange(GRID_W), rows).astype(jnp.float32)
    half = ATT_QK_DIM // 2
    inv = ROPE_BASE ** (-jnp.arange(0, half, 2, dtype=jnp.float32) / half)
    return row[:, None] * inv, col[:, None] * inv

def rope_rotate(x, ang):
    x1, x2 = jnp.split(x, 2, axis=-1)
    cos = jnp.cos(ang).astype(x.dtype)
    sin = jnp.sin(ang).astype(x.dtype)
    return jnp.concatenate([x1 * cos - x2 * sin, x2 * cos + x1 * sin], axis=-1)

def apply_axial_rope(x, ang_row, ang_col):
    half = ATT_QK_DIM // 2
    ar = ang_row[None, :, None, None, :]
    ac = ang_col[None, :, None, None, :]
    return jnp.concatenate([rope_rotate(x[..., :half], ar), rope_rotate(x[..., half:], ac)], axis=-1)

def diff_attention(q, k, v, lam):
    b, nq = q.shape[:2]
    nblk = nq // Q_BLOCK
    qb = jnp.moveaxis(q.reshape(b, nblk, Q_BLOCK, ATT_HEADS, 2, ATT_QK_DIM), 1, 0)
    scale = ATT_QK_DIM ** -0.5

    def block(qi):
        s = jnp.einsum('bqhmd,bkhmd->bhmqk', qi, k, preferred_element_type=jnp.float32) * scale
        p = jax.nn.softmax(s, axis=-1)
        a = p[:, :, 0] - lam * p[:, :, 1]
        return jnp.einsum('bhqk,bkhd->bqhd', a.astype(v.dtype), v)

    o = lax.map(block, qb)
    return jnp.moveaxis(o, 0, 1).reshape(b, nq, ATT_HEADS, ATT_V_DIM)

def segsum(a):
    q = a.shape[-1]
    x = jnp.broadcast_to(a[..., None], a.shape + (q,))
    x = jnp.where(jnp.tril(jnp.ones((q, q), bool), -1), x, 0.0)
    s = jnp.cumsum(x, axis=-2)
    return jnp.where(jnp.tril(jnp.ones((q, q), bool)), s, -jnp.inf)

def ssd_chunked_scan(x, dt, a, bm, cm, h0):
    b, n, h, pdim = x.shape
    nc, q = n // SSD_CHUNK, SSD_CHUNK
    xdt = (x.astype(jnp.float32) * dt[..., None]).reshape(b, nc, q, h, pdim)
    bc = bm.astype(jnp.float32).reshape(b, nc, q, h, SSD_STATE)
    cc = cm.astype(jnp.float32).reshape(b, nc, q, h, SSD_STATE)
    adt = (dt * a).reshape(b, nc, q, h).transpose(0, 3, 1, 2)
    a_cs = jnp.cumsum(adt, axis=-1)
    decay_in = jnp.exp(segsum(adt))
    y_diag = jnp.einsum('bclhn,bcshn,bhcls,bcshp->bclhp', cc, bc, decay_in, xdt)
    decay_to_end = jnp.exp(a_cs[..., -1:] - a_cs)
    chunk_states = jnp.einsum('bclhn,bhcl,bclhp->bchpn', bc, decay_to_end, xdt)
    chunk_decay = jnp.exp(a_cs[..., -1])

    def step(state, inp):
        st, dec = inp
        return state * dec[..., None, None] + st, state

    h_final, h_enter = lax.scan(step, h0.astype(jnp.float32),
                                (jnp.moveaxis(chunk_states, 1, 0), jnp.moveaxis(chunk_decay, 2, 0)))
    h_enter = jnp.moveaxis(h_enter, 0, 1)
    y_off = jnp.einsum('bclhn,bchpn,bhcl->bclhp', cc, h_enter, jnp.exp(a_cs))
    return (y_diag + y_off).reshape(b, n, h, pdim), h_final

def ssd_mixer(z, xbc, dt_raw, p, h0_f, h0_b):
    b, n, _ = xbc.shape
    xbc = jax.nn.silu(dwconv_centred(xbc, p['ssd_conv_w'], p['ssd_conv_b']))
    xs, bs, cs = split_sizes(xbc, (SSD_DIM, SSD_GROUPS * SSD_STATE, SSD_GROUPS * SSD_STATE))
    rep = SSD_HEADS // SSD_GROUPS
    x = xs.reshape(b, n, SSD_HEADS, SSD_HEAD_DIM)
    bm = jnp.repeat(bs.reshape(b, n, SSD_GROUPS, SSD_STATE), rep, axis=2)
    cm = jnp.repeat(cs.reshape(b, n, SSD_GROUPS, SSD_STATE), rep, axis=2)
    dt = jax.nn.softplus(dt_raw.astype(jnp.float32).reshape(b, n, 2, SSD_HEADS)
                         + p['ssd_dt_bias'].astype(jnp.float32))
    a = -jnp.exp(p['ssd_A_log'].astype(jnp.float32))
    y_f, h_f = ssd_chunked_scan(x, dt[:, :, 0], a[0], bm, cm, h0_f)
    flip = lambda t: jnp.flip(t, axis=1)
    y_b, h_b = ssd_chunked_scan(flip(x), flip(dt[:, :, 1]), a[1], flip(bm), flip(cm), h0_b)
    y = y_f + flip(y_b) + p['ssd_D'].astype(jnp.float32)[:, None] * x.astype(jnp.float32)
    yz = y.reshape(b, n, SSD_DIM) * jax.nn.silu(z.astype(jnp.float32))
    yz = yz.reshape(b, n, SSD_GROUPS, SSD_DIM // SSD_GROUPS)
    yz = yz * lax.rsqrt(jnp.mean(yz * yz, axis=-1, keepdims=True) + EPS)
    out = yz.reshape(b, n, SSD_DIM) * p['ssd_norm_g'].astype(jnp.float32)
    return out.astype(z.dtype), h_f, h_b

def trunk_layer(x, mod, p, lidx, rope_ang, ctx_kv, h0):
    b, n, _ = x.shape
    sh1, sc1, g1, sh2, sc2, g2 = jnp.split(mod[:, None, :].astype(x.dtype), N_MOD, axis=-1)
    h = rmsnorm(x, p['norm1_g']) * (1 + sc1) + sh1
    u, q, k, v, z, xbc, dt_raw = split_sizes(h @ p['w_in'], IN_SIZES)

    o_pool = multiscale_pool_mixer(u, p['pool_w'], p['pool_scale'])

    q = q.reshape(b, n, ATT_HEADS, 2, ATT_QK_DIM)
    k = k.reshape(b, n, ATT_HEADS, 2, ATT_QK_DIM)
    v = v.reshape(b, n, ATT_HEADS, ATT_V_DIM)
    if ctx_kv is None:
        k_keys, v_keys = k, v
    else:
        ang_r, ang_c = rope_ang
        q = apply_axial_rope(q, ang_r, ang_c)
        k_keys = jnp.concatenate([ctx_kv[0].astype(k.dtype), apply_axial_rope(k, ang_r, ang_c)], axis=1)
        v_keys = jnp.concatenate([ctx_kv[1].astype(v.dtype), v], axis=1)
    lam_init = 0.8 - 0.6 * math.exp(-0.3 * lidx)
    lp = p['att_lambda'].astype(jnp.float32)
    lam = jnp.exp(jnp.sum(lp[0] * lp[1])) - jnp.exp(jnp.sum(lp[2] * lp[3])) + lam_init
    o_att = diff_attention(q, k_keys, v_keys, lam)
    o_att = (rmsnorm(o_att, p['att_subln_g']) * (1 - lam_init)).reshape(b, n, ATT_DIM)

    o_ssd, h_f, h_b = ssd_mixer(z, xbc, dt_raw, p, h0[0], h0[1])

    gate_pool, gate_att, gate_ssd = jnp.split(jax.nn.sigmoid(h @ p['w_gate'] + p['b_gate']), 3, axis=-1)
    wb_pool, wb_att, wb_ssd = split_sizes(p['w_branch'], (POOL_DIM, ATT_DIM, SSD_DIM), axis=0)
    merged = gate_pool * (o_pool @ wb_pool) + gate_att * (o_att @ wb_att) + gate_ssd * (o_ssd @ wb_ssd)
    x = x + g1 * (merged @ p['w_out'])

    h2 = rmsnorm(x, p['norm2_g']) * (1 + sc2) + sh2
    up = dwconv_centred(h2 @ p['ffn_w_up'], p['ffn_conv_w'], p['ffn_conv_b'])
    a_gate, a_val = jnp.split(up, 2, axis=-1)
    x = x + g2 * ((jax.nn.silu(a_gate) * a_val) @ p['ffn_w_down'])
    return x, k, v, h_f, h_b

def setup_inputs(seed: int = 0) -> dict:
    key = jax.random.key(seed)
    keys = list(jax.random.split(key, 40))
    f32 = jnp.float32

    def nrm(shape, scale):
        return scale * jax.random.normal(keys.pop(), shape, f32)

    dt_init = jnp.exp(jax.random.uniform(keys.pop(), (DEPTH, 2, SSD_HEADS), f32,
                                         math.log(1e-3), math.log(1e-1)))
    a_init = jax.random.uniform(keys.pop(), (DEPTH, 2, SSD_HEADS), f32, 1.0, 16.0)
    return {
        'x_prompt': nrm((BATCH, SEQ, D_MODEL), 1.0),
        'x_sample': nrm((DEC_BATCH, DEC_SEQ, D_MODEL), 1.0),
        'c': nrm((DEC_BATCH, D_MODEL), 1.0),
        'cache_attn_k': nrm((DEC_BATCH, DEPTH, PAST_LEN, ATT_HEADS, 2, ATT_QK_DIM), 1.0),
        'cache_attn_v': nrm((DEC_BATCH, DEPTH, PAST_LEN, ATT_HEADS, ATT_V_DIM), 1.0),
        'state_ssd': nrm((DEC_BATCH, DEPTH, 2, SSD_HEADS, SSD_HEAD_DIM, SSD_STATE), 0.1),
        'c_ctx': nrm((D_MODEL,), 1.0),
        'w_mod': nrm((DEPTH, D_MODEL, N_MOD * D_MODEL), 0.5 * D_MODEL ** -0.5),
        'b_mod': nrm((DEPTH, N_MOD * D_MODEL), 0.02),
        'norm1_g': 1.0 + nrm((DEPTH, D_MODEL), 0.05),
        'w_in': nrm((DEPTH, D_MODEL, IN_DIM), D_MODEL ** -0.5),
        'pool_w': nrm((DEPTH, POOL_GROUPS, POOL_GROUP_DIM, POOL_GROUP_DIM), POOL_GROUP_DIM ** -0.5),
        'pool_scale': 1.0 + nrm((DEPTH, POOL_DIM), 0.1),
        'att_lambda': nrm((DEPTH, 4, ATT_QK_DIM), 0.1),
        'att_subln_g': 1.0 + nrm((DEPTH, ATT_V_DIM), 0.05),
        'ssd_conv_w': nrm((DEPTH, SSD_CONV_W, SSD_XBC_DIM), SSD_CONV_W ** -0.5),
        'ssd_conv_b': nrm((DEPTH, SSD_XBC_DIM), 0.02),
        'ssd_dt_bias': dt_init + jnp.log(-jnp.expm1(-dt_init)),
        'ssd_A_log': jnp.log(a_init),
        'ssd_D': 1.0 + nrm((DEPTH, SSD_HEADS), 0.1),
        'ssd_norm_g': 1.0 + nrm((DEPTH, SSD_DIM), 0.05),
        'w_gate': nrm((DEPTH, D_MODEL, 3 * D_MODEL), D_MODEL ** -0.5),
        'b_gate': nrm((DEPTH, 3 * D_MODEL), 0.02),
        'w_branch': nrm((DEPTH, MIX_DIM, D_MODEL), POOL_DIM ** -0.5),
        'w_out': nrm((DEPTH, D_MODEL, D_MODEL), D_MODEL ** -0.5),
        'norm2_g': 1.0 + nrm((DEPTH, D_MODEL), 0.05),
        'ffn_w_up': nrm((DEPTH, D_MODEL, 2 * FFN_DIM), D_MODEL ** -0.5),
        'ffn_conv_w': nrm((DEPTH, FFN_CONV_W, 2 * FFN_DIM), FFN_CONV_W ** -0.5),
        'ffn_conv_b': nrm((DEPTH, 2 * FFN_DIM), 0.02),
        'ffn_w_down': nrm((DEPTH, FFN_DIM, D_MODEL), FFN_DIM ** -0.5),
        'final_norm_g': 1.0 + nrm((D_MODEL,), 0.05),
    }

def reference(x_prompt, x_sample, c, cache_attn_k, cache_attn_v, state_ssd, c_ctx, w_mod, b_mod,
              norm1_g, w_in, pool_w, pool_scale, att_lambda, att_subln_g, ssd_conv_w, ssd_conv_b,
              ssd_dt_bias, ssd_A_log, ssd_D, ssd_norm_g, w_gate, b_gate, w_branch, w_out, norm2_g,
              ffn_w_up, ffn_conv_w, ffn_conv_b, ffn_w_down, final_norm_g):
    params = [dict(norm1_g=norm1_g[l], w_in=w_in[l], pool_w=pool_w[l], pool_scale=pool_scale[l],
                   att_lambda=att_lambda[l], att_subln_g=att_subln_g[l], ssd_conv_w=ssd_conv_w[l],
                   ssd_conv_b=ssd_conv_b[l], ssd_dt_bias=ssd_dt_bias[l], ssd_A_log=ssd_A_log[l],
                   ssd_D=ssd_D[l], ssd_norm_g=ssd_norm_g[l], w_gate=w_gate[l], b_gate=b_gate[l],
                   w_branch=w_branch[l], w_out=w_out[l], norm2_g=norm2_g[l], ffn_w_up=ffn_w_up[l],
                   ffn_conv_w=ffn_conv_w[l], ffn_conv_b=ffn_conv_b[l], ffn_w_down=ffn_w_down[l])
              for l in range(DEPTH)]

    xp = x_prompt
    h0_zero = jnp.zeros((x_prompt.shape[0], SSD_HEADS, SSD_HEAD_DIM, SSD_STATE), jnp.float32)
    new_k, new_v, new_s = [], [], []
    for l in range(DEPTH):
        mod_ctx = jax.nn.silu(c_ctx)[None, :] @ w_mod[l] + b_mod[l]
        xp, k_l, v_l, hf_l, hb_l = trunk_layer(xp, mod_ctx, params[l], l, None, None, (h0_zero, h0_zero))
        new_k.append(k_l)
        new_v.append(v_l)
        new_s.append(jnp.stack([hf_l, hb_l], axis=1))

    xs = x_sample
    rope_ang = axial_rope_angles(x_sample.shape[1])
    for l in range(DEPTH):
        mod_lat = jax.nn.silu(c) @ w_mod[l] + b_mod[l]
        xs = trunk_layer(xs, mod_lat, params[l], l, rope_ang,
                         (cache_attn_k[:, l], cache_attn_v[:, l]),
                         (state_ssd[:, l, 0], state_ssd[:, l, 1]))[0]

    y_prompt = rmsnorm(xp, final_norm_g)
    y_sample = rmsnorm(xs, final_norm_g)
    new_cache_attn_k = jnp.stack(new_k, axis=1)
    new_cache_attn_v = jnp.stack(new_v, axis=1)
    new_state_ssd = jnp.stack(new_s, axis=1)
    return (y_prompt, y_sample, new_cache_attn_k, new_cache_attn_v, new_state_ssd)


_drawn_inputs = setup_inputs


def setup_inputs(seed=0):
    import zlib

    import numpy as np

    out = dict(_drawn_inputs(seed))
    spreads = {}
    factors = {'pool_scale': 2.791,
     'att_lambda': 4.583,
     'att_subln_g': 6.529,
     'ssd_D': 5.996,
     'ssd_norm_g': 5.215,
     'b_gate': 8.0,
     'norm2_g': 2.805,
     'ffn_conv_b': 7.504}
    for name, (base, spread) in spreads.items():
        noise = np.random.default_rng([zlib.crc32(name.encode()), seed]).standard_normal(out[name].shape)
        drawn = base * np.exp(spread * noise) if base else spread * noise
        out[name] = __import__('jax').numpy.asarray(drawn.astype(out[name].dtype))
    for name, factor in factors.items():
        out[name] = (out[name] * factor).astype(out[name].dtype)
    return out
```

```python
from contextlib import ExitStack

import numpy as np

import concourse.bass as bass
from concourse import mybir

F32 = mybir.dt.float32
F32R = mybir.dt.float32r
ALU = mybir.AluOpType
ACT = mybir.ActivationFunctionType
AX = mybir.AxisListType

P = 128
D = 1024
KT = D // P
DEPTH = 2
SEQ, LAT, PAST = 128, 256, 128
GRID_W = 64
EPS = 1e-6
GAP = 2
CTX0 = LAT + GAP
T = CTX0 + SEQ
SEGS = ((0, LAT), (CTX0, T))
CHUNK0 = (0, P, CTX0)
NCH = 3
HEADS = 4
QK = 64
SCALE = QK ** -0.5
SSD_H, SSD_P, SSD_G = 8, 64, 2
WINDOWS = (2, 4, 8, 16)
PADL = 8
ULAT, UCTX = PADL, PADL + LAT + 2 * PADL
UW = UCTX + SEQ + PADL
FFN = ((8 * D // 3 + 127) // 128) * 128
FT = FFN // P
NEG = -1e30

XBC, UU, QQ, KK, VV, ZZ, GATE, BRANCH, OUT, UP, DOWN = (
    "xbc", "u", "q", "k", "v", "z", "gate", "branch", "out", "up", "down")
GROUPS = ([(XBC, j) for j in range(8)] + [(UU, j) for j in range(4)] + [(QQ, j) for j in range(4)]
          + [(KK, j) for j in range(4)] + [(VV, c) for c in range(NCH)] + [(ZZ, j) for j in range(4)]
          + [(GATE, j) for j in range(24)] + [(BRANCH, j) for j in range(24)]
          + [(OUT, j) for j in range(8)] + [(UP, j) for j in range(2 * FT)] + [(DOWN, j) for j in range(8)])
NG = len(GROUPS)
G_OF = {g: i for i, g in enumerate(GROUPS)}
BANKS = 4
DOWN_CUTS = ((0, 8), (8, 15), (15, FT))

UNITS = ([(XBC, j, 0) for j in range(8)] + [(UU, j, 0) for j in range(4)] + [(QQ, j, 0) for j in range(4)]
         + [(KK, j, 0) for j in range(4)] + [(VV, 0, v) for v in range(4)] + [(ZZ, j, 0) for j in range(4)]
         + [(GATE, j, 0) for j in range(24)] + [(BRANCH, j, 0) for j in range(0, 24, 2)]
         + [(OUT, j, 0) for j in range(8)] + [(UP, j, 0) for j in range(2 * FT)]
         + [(DOWN, j, c) for j in range(8) for c in range(3)])
NU = len(UNITS)
U_OF = {u: i for i, u in enumerate(UNITS)}
AHEAD = 3
NRAW, NMOD, NHL = 4, 2, 3
MODT = 6 * KT
MOD_HEAD = 2 * KT
MOD_FIRST = 4
MIX0 = U_OF[(ZZ, 0, 0)]


def closing_unit(g):
    kind, j = GROUPS[g]
    return U_OF[{VV: (VV, 0, 3), BRANCH: (BRANCH, j - j % 2, 0), DOWN: (DOWN, j, 2)}.get(kind, (kind, j, 0))]


def done_after(u):
    kind, j, part = UNITS[u]
    if kind == VV:
        return [G_OF[(VV, c)] for c in range(NCH)] if part == 3 else []
    if kind == BRANCH:
        return [G_OF[(BRANCH, j)], G_OF[(BRANCH, j + 1)]]
    if kind == DOWN:
        return [G_OF[(DOWN, j)]] if part == 2 else []
    return [G_OF[(kind, j)]]


def mod_after(u):
    m = MOD_HEAD + 2 * (u - MOD_FIRST)
    return [m, m + 1] if MOD_HEAD <= m < MODT else []


def stream_order():
    order = [("w", u) for u in range(NRAW)] + [("mod", m) for m in range(MOD_HEAD)]
    order += [("w", u) for u in range(NRAW, AHEAD + MOD_FIRST)]
    for u in range(AHEAD + MOD_FIRST, NU + AHEAD):
        if u < NU:
            order.append(("w", u))
        order += [("mod", m) for m in mod_after(u - AHEAD)]
    return order


STREAM = stream_order()
NS = len(STREAM)
COLS = {}
for _u, (_k, _j, _c) in enumerate(UNITS):
    COLS[_u] = P * (DOWN_CUTS[_c][1] - DOWN_CUTS[_c][0]) if _k == DOWN else P * KT

PAR = {}
_at = 0
for _name, _n in (("bmod", MODT), ("n1g", KT), ("n2g", KT), ("pscale", 4), ("subg", 1), ("li", 1), ("oml", 1),
                  ("cw", 24), ("cb", 8), ("ssdg", 4), ("ssdD", 4), ("bgate", 24), ("fw", 6 * FT), ("fb", 2 * FT),
                  ("dtb", 16), ("alog", 16), ("lam", 4 * QK), ("wdt", KT * 16), ("plw", 4 * P)):
    PAR[_name] = (_at, _n)
    _at += _n
NPAR = _at

TAB = {}
_at = 0
for _name, _n in (("ident", P), ("ones", P), ("le", P), ("ge", P), ("gt", P), ("lt", P), ("negf", P), ("negb", P),
                  ("cos", LAT), ("sin", LAT), ("edge", 64), ("eps", 1)):
    TAB[_name] = (_at, _n)
    _at += _n
NTAB = _at

NATT = HEADS * NCH
NY = NCH * SSD_G
NMISC = 14
NCONV = 8 + 2 * FT
M_DT, M_SM, M_PW, M_ATT, M_SSD, M_N2 = 1, 2, 3, 7, 11, 13
S_TASKS = ((0, 0), (1, 1), (2, 0), (2, 1))
SLOT_PW, SLOT_X, SLOT_S, SLOT_Y = 4, 14, 17, 21
SLOT_RMS = SLOT_Y + NY + 1


def count(l, per, i):
    return l * per + i + 1


class Steps:

    def __init__(self, eng, sem):
        self.eng, self.sem, self.n = eng, sem, 0

    def then(self, ins):
        ins.then_inc(self.sem, 1)
        self.n += 1
        self.eng.wait_ge(self.sem, self.n)


def tables():
    t = np.zeros((P, NTAB), np.float32)

    def put(name, a):
        at, n = TAB[name]
        t[:, at:at + n] = a

    i, j = np.arange(P)[:, None], np.arange(P)[None, :]
    put("ident", i == j)
    put("ones", 1.0)
    put("le", i <= j)
    put("ge", i >= j)
    put("gt", i > j)
    put("lt", i < j)
    put("negf", np.where(j >= i, 0.0, NEG))
    put("negb", np.where(j <= i, 0.0, NEG))
    tok = np.arange(LAT)
    half = QK // 2
    inv = (np.float32(10000.0) ** (-np.arange(0, half, 2, dtype=np.float32) / np.float32(half))).astype(np.float32)
    ang = np.zeros((P, LAT), np.float32)
    sign = np.zeros((P, 1), np.float32)
    for p in range(P):
        d = p % QK
        pos = (tok // GRID_W if d < half else tok % GRID_W).astype(np.float32)
        ang[p] = pos * inv[d % (half // 2)]
        sign[p] = -1.0 if d % half < half // 2 else 1.0
    put("cos", np.cos(ang))
    put("sin", np.sin(ang) * sign)
    edge = np.zeros((4, 2, PADL), np.float32)
    for g, w in enumerate(WINDOWS):
        h = w // 2
        for k in range(PADL):
            edge[g, 0, k] = 1.0 / (min(k, h) + h)
            tail = PADL - k
            edge[g, 1, k] = 1.0 / (min(tail, h) + h)
    put("edge", edge.reshape(1, 64))
    put("eps", EPS)
    return t


def build(nc, wstream, par, tab, xs, xp, cvec, kc, vc, st0, fng, y, newk, newv, news):
    ctx = ExitStack()
    with ctx:
        def sb(name, shape, dt=F32, where=ctx):
            return where.enter_context(nc.sbuf_tensor(name, shape, dt))

        def sem(name):
            return ctx.enter_context(nc.semaphore(name))

        raw = sb("raw", [P, NRAW, P * KT])
        rawm = sb("rawm", [P, NMOD, P * KT])
        wh = sb("wh", [P, NHL, P * KT], F32R)
        wl = sb("wl", [P, NHL, P * KT], F32R)
        x = sb("x", [P, KT, T])
        hh = sb("hh", [P, KT, T], F32R)
        hl = sb("hl", [P, KT, T], F32R)
        with ExitStack() as a:
            gates = sb("gates", [P, 24, T], where=a)
            xbc = sb("xbc", [P, 8, T], where=a)
            zz = sb("zz", [P, 4, T], where=a)
            ut = sb("ut", [P, 4, UW], where=a)
            ot = sb("ot", [P, HEADS, T], where=a)
        with ExitStack() as a:
            sb("under_gates", [P, 24, T], where=a)
            osh = sb("osh", [P, 4, T], F32R, where=a)
            osl = sb("osl", [P, 4, T], F32R, where=a)
        with ExitStack() as a:
            ah = sb("ah", [P, FT, T], F32R, where=a)
            al = sb("al", [P, FT, T], F32R, where=a)
        sb("main_region", [P, 24 * T + 8 * T + 4 * T + 4 * UW + HEADS * T])
        with ExitStack() as a:
            qt = sb("qt", [P, HEADS, T], where=a)
            kt_ = sb("kt", [P, HEADS, PAST + T], where=a)
            vv = sb("vv", [P, 4, 4 * P], where=a)
            pr = sb("pr", [P, 2, 2, PAST + LAT], where=a)
            at_ = sb("at", [P, 2, PAST + LAT], where=a)
        with ExitStack() as a:
            xt = sb("xt", [P, NCH, 4 * P], where=a)
            bg = sb("bg", [P, NCH, 4 * P], where=a)
            hst = sb("hst", [P, 4, 4 * P], where=a)
            xw = sb("xw", [P, 4 * P], where=a)
            with ExitStack() as b:
                rst = sb("rst", [P, 4, T], where=b)
            ee = sb("ee", [P, 2, 4 * P], where=a)
            eb = sb("eb", [P, 2, 4 * P], where=a)
        with ExitStack() as a:
            mh = sb("mh", [P, KT, T], F32R, where=a)
            ml = sb("ml", [P, KT, T], F32R, where=a)
        sb("mixer_region", [P, 2 * HEADS * T + HEADS * PAST + 16 * P + 6 * (PAST + LAT)])
        cv = sb("cv", [P, 2, T])
        th = sb("th", [P, 2, T])
        sqa = sb("sqa", [P, T])
        rs = sb("rs", [P, T])
        prm = sb("prm", [P, NPAR])
        tb = sb("tb", [P, NTAB])
        wdh = sb("wdh", [P, KT * 16], F32R)
        wdl = sb("wdl", [P, KT * 16], F32R)
        mod = sb("mod", [P, MODT, 2])
        sc1 = sb("sc1", [P, KT, 2])
        sc2 = sb("sc2", [P, KT, 2])
        g1h = sb("g1h", [P, KT, 2])
        cs = sb("cs", [P, 2 * KT])
        csh = sb("csh", [P, 2 * KT])
        cst = sb("cst", [P, 2 * KT])
        bgh = sb("bgh", [P, 24])
        nlam = sb("nlam", [P, 1])
        lamt = sb("lamt", [P, 2, QK])
        lams = sb("lams", [P, 4])
        sg = sb("sg", [P, 1])
        eal = sb("eal", [P, 16])
        mxb = sb("mxb", [P, 2, 2])
        nmb = sb("nmb", [P, 2, 2])
        rsm = sb("rsm", [P, 2, 2])
        rcp = sb("rcp", [P, 3])
        dtv = sb("dtv", [P, 48])
        dte = sb("dte", [P, 48])
        dtt = sb("dtt", [P, 48])
        adt = sb("adt", [P, 48])
        sm = sb("sm", [P, 144])
        nac = sb("nac", [P, 48])
        ede = sb("ede", [P, 96])
        wdc = sb("wdc", [P, 48])
        fg = sb("fg", [P, KT])

        acc = [ctx.enter_context(nc.psum_tensor(f"acc{i}", [P, 512], F32)) for i in range(BANKS)]
        misc = ctx.enter_context(nc.psum_tensor("misc", [P, 512], F32))
        mix5 = ctx.enter_context(nc.psum_tensor("mix5", [P, 512], F32))
        mix6 = ctx.enter_context(nc.psum_tensor("mix6", [P, 512], F32))
        mix7 = ctx.enter_context(nc.psum_tensor("mix7", [P, 512], F32))
        modp = mix7[:, 0:2 * MODT]
        mz = misc[:, 0:T]

        def prm_(name, i=0, n=1):
            at = PAR[name][0] + i
            return prm[:, at:at + n]

        def tab_(name):
            at, n = TAB[name]
            return tb[:, at:at + n]

        ident, ones, le, ge, gt, lt = (tab_(n) for n in ("ident", "ones", "le", "ge", "gt", "lt"))
        tri, neg = (le, ge), (tab_("negf"), tab_("negb"))
        cos, sin = tab_("cos"), tab_("sin")
        edge = tab_("edge").rearrange("p (g s k) -> p g s k", g=4, s=2)

        tab_in = sem("tab_in")
        par_in = sem("par_in")
        cache_in = sem("cache_in")
        state_in = sem("state_in")
        raw_in = [sem(f"raw_in{i}") for i in range(NRAW)]
        mod_in = [sem(f"mod_in{i}") for i in range(NMOD)]
        hi_done = sem("hi_done")
        lo_done = sem("lo_done")
        unit_used = sem("unit_used")
        mod_used = sem("mod_used")
        cs_ready = sem("cs_ready")
        cs_tanh = sem("cs_tanh")
        cs_half = sem("cs_half")
        mod_read = sem("mod_read")
        misc_done = sem("misc_done")
        att_ss = sem("att_ss")
        z_ss = sem("z_ss")
        zeroed = sem("zeroed")
        sq_done = sem("sq_done")
        sq_sum = sem("sq_sum")
        rs_ready = sem("rs_ready")
        h_full = sem("h_full")
        h_hi = sem("h_hi")
        h_lo = sem("h_lo")
        x_new = sem("x_new")
        cv_init = sem("cv_init")
        cv_done = sem("cv_done")
        cv_tanh = sem("cv_tanh")
        cv_out = sem("cv_out")
        par_ready = sem("par_ready")
        lam_exp = sem("lam_exp")
        lam_sum = sem("lam_sum")
        wd_hi = sem("wd_hi")
        u_in = sem("u_in")
        pooled = sem("pooled")
        pads = sem("pads")
        op_done = sem("op_done")
        qk_in = sem("qk_in")
        qk_done = sem("qk_done")
        v_in = sem("v_in")
        z_tanh = sem("z_tanh")
        z_done = sem("z_done")
        dt_raw = sem("dt_raw")
        dt_log = sem("dt_log")
        adt_done = sem("adt_done")
        sm_done = sem("sm_done")
        ede_done = sem("ede_done")
        wdc_done = sem("wdc_done")
        s_done = sem("s_done")
        nm_done = sem("nm_done")
        exp_done = sem("exp_done")
        a_done = sem("a_done")
        tr_done = sem("tr_done")
        at_done = sem("at_done")
        av_done = sem("av_done")
        o_done = sem("o_done")
        osq_done = sem("osq_done")
        ors_done = sem("ors_done")
        on_done = sem("on_done")
        xt_done = sem("xt_done")
        xt_in = sem("xt_in")
        xw_done = sem("xw_done")
        cst_done = sem("cst_done")
        st_done = sem("st_done")
        bc_done = sem("bc_done")
        d_done = sem("d_done")
        e_done = sem("e_done")
        m_done = sem("m_done")
        y_done = sem("y_done")
        yz_done = sem("yz_done")
        zsq_done = sem("zsq_done")
        zrs_done = sem("zrs_done")
        zn_done = sem("zn_done")
        g_done = sem("g_done")
        gb_done = sem("gb_done")
        mg_done = sem("mg_done")
        k_out = sem("k_out")
        v_out = sem("v_out")
        st_out = sem("st_out")
        y_ready = sem("y_ready")
        y_out = sem("y_out")
        dve_step = sem("dve_step")
        act_step = sem("act_step")
        pool_step = sem("pool_step")

        SP_N1, SP_OP, SP_OT, SP_Z, SP_MG, SP_N2, SP_FF = 0, 8, 12, 16, 20, 28, 36
        NSPLIT = SP_FF + FT
        F_N1, F_MG, F_N2, F_FF = 0, 8, 16, 24
        NFULL = F_FF + FT

        def raw_slot(u):
            return u % NRAW

        def raw_value(l, u):
            return 16 * (l * (NU // NRAW) + u // NRAW + 1)

        def mod_value(l, m):
            return 16 * (l * (MODT // NMOD) + m // NMOD + 1)

        def group_done(eng, l, g):
            eng.wait_ge(unit_used, count(l, NU, closing_unit(g)))

        def group_read(eng, l, g):
            kind, j = GROUPS[g]
            s_, per, i = {XBC: (cv_done, NCONV, j), UP: (cv_done, NCONV, 8 + j), UU: (u_in, 4, j), QQ: (qk_in, 8, j),
                          KK: (qk_in, 8, HEADS + j), VV: (v_in, NCH, j), ZZ: (z_done, 4, j), GATE: (g_done, 24, j),
                          BRANCH: (gb_done, 24, j), OUT: (x_new, 16, j), DOWN: (x_new, 16, KT + j)}[kind]
            eng.wait_ge(s_, count(l, per, i))

        def misc_read(eng, l, i):
            if i == 0 or i == M_N2:
                eng.wait_ge(rs_ready, count(l, 2, i == M_N2))
            elif i == M_DT:
                eng.wait_ge(dt_raw, l + 1)
            elif i == M_SM:
                eng.wait_ge(sm_done, l + 1)
            elif i < M_ATT:
                eng.wait_ge(op_done, count(l, 4, i - M_PW))
            elif i < M_SSD:
                eng.wait_ge(att_ss, count(l, HEADS, i - M_ATT))
            else:
                eng.wait_ge(z_ss, count(l, 2, i - M_SSD))

        block = ctx.enter_context(nc.Block())

        @block.sync
        def _(sp):
            for l in range(DEPTH):
                for i, (kind, n) in enumerate(STREAM):
                    if kind == "w":
                        if l or n >= NRAW:
                            sp.wait_ge(lo_done, l * NU + n - NRAW + 1)
                        sp.dma_start(raw[:, raw_slot(n), 0:COLS[n]], wstream[l, i, :, 0:COLS[n]]) \
                            .then_inc(raw_in[raw_slot(n)], 16)
                    else:
                        if l or n >= NMOD:
                            sp.wait_ge(mod_used, l * MODT + n - NMOD + 1)
                        sp.dma_start(rawm[:, n % NMOD, :], wstream[l, i, :, :]).then_inc(mod_in[n % NMOD], 16)

        @block.gpsimd
        def _(pool):
            step = Steps(pool, pool_step)
            for dst, src in ((x[:, :, 0:LAT], xs), (x[:, :, CTX0:T], xp), (cs[:, :], cvec), (tb[:, :], tab),
                             (fg[:, :], fng)):
                pool.dma_start(dst, src).then_inc(tab_in, 16)
            nc.gpsimd.memset(x[:, :, LAT:CTX0], 0.0).then_inc(zeroed, 1)
            nc.gpsimd.memset(cv[:, :, :], 0.0).then_inc(zeroed, 1)

            def sum_squares(l, first, base):
                for j in range(KT):
                    pool.wait_ge(sq_done, base + j + 1)
                    if j == 0:
                        if not first:
                            pool.wait_ge(misc_done, count(l, NMISC, 0))
                        nc.gpsimd.tensor_copy(sqa[:, :], th[:, 0, :]).then_inc(sq_sum, 1)
                    else:
                        pool.wait_ge(sq_sum, base + j)
                        nc.gpsimd.tensor_tensor(sqa[:, :], sqa[:, :], th[:, j % 2, :], ALU.add).then_inc(sq_sum, 1)

            sum_squares(0, True, 0)

            def load_params(l):
                pool.dma_start(prm[:, :], par[l]).then_inc(par_in, 16)

            load_params(0)
            for l in range(DEPTH):
                if l:
                    group_done(pool, l - 1, G_OF[(OUT, KT - 1)])
                pool.dma_start(kt_[:, :, 0:PAST], kc[l]).then_inc(cache_in, 16)
                pool.dma_start(vv[:, 0, :], vc[l]).then_inc(cache_in, 16)
                if l:
                    group_done(pool, l - 1, NG - 1)
                for c0, c1 in ((0, PADL), (ULAT + LAT, UCTX), (UCTX + SEQ, UW)):
                    nc.gpsimd.memset(ut[:, :, c0:c1], 0.0)
                nc.gpsimd.memset(gates[:, 16:20, LAT:CTX0], 0.0)
                nc.gpsimd.memset(ot[:, :, LAT:CTX0], 0.0).then_inc(pads, 1)
                pool.wait_ge(pads, l + 1)
                tmp = [gates[:, 20:22, :].rearrange("p a t -> p (a t)")[:, 0:UW],
                       gates[:, 22:24, :].rearrange("p a t -> p (a t)")[:, 0:UW]]
                for j in range(4):
                    pool.wait_ge(u_in, count(l, 4, j))
                    step.then(nc.gpsimd.tensor_tensor(tmp[0][:, 1:UW], ut[:, j, 0:UW - 1], ut[:, j, 1:UW], ALU.add))
                    lo, cur = 1, 0
                    for i in range(j):
                        s = 1 << i
                        lo += s
                        hi = UW - (lo - 1)
                        step.then(nc.gpsimd.tensor_tensor(tmp[1 - cur][:, lo:hi], tmp[cur][:, lo - s:hi - s],
                                                          tmp[cur][:, lo + s:hi + s], ALU.add))
                        cur = 1 - cur
                    win = tmp[cur]
                    out = gates[:, 16 + j, :]
                    for (a, b), u0 in zip(SEGS, (ULAT, UCTX)):
                        n = b - a
                        step.then(nc.gpsimd.tensor_scalar(out[:, a:b], win[:, u0:u0 + n], 1.0 / WINDOWS[j], None, ALU.mult))
                        nc.gpsimd.tensor_tensor(out[:, a:a + PADL], win[:, u0:u0 + PADL], edge[:, j, 0, :], ALU.mult)
                        step.then(nc.gpsimd.tensor_tensor(out[:, b - PADL:b], win[:, u0 + n - PADL:u0 + n],
                                                          edge[:, j, 1, :], ALU.mult))
                        ins = nc.gpsimd.tensor_tensor(out[:, a:b], out[:, a:b], ut[:, j, u0:u0 + n], ALU.subtract)
                        if a == 0:
                            step.then(ins)
                        else:
                            ins.then_inc(pooled, 1)
                for i in range(HEADS):
                    pool.wait_ge(qk_done, count(l, 2 * HEADS, HEADS + i))
                pool.dma_start(newk[l], kt_[:, :, PAST + CTX0:PAST + T]).then_inc(k_out, 16)
                pool.wait_ge(v_in, count(l, NCH, NCH - 1))
                pool.dma_start(newv[l], vv[:, 3, :]).then_inc(v_out, 16)
                pool.wait_ge(av_done, count(l, NATT, NATT - 1))
                pool.wait_ge(k_out, 16 * (l + 1))
                pool.wait_ge(v_out, 16 * (l + 1))
                for d in range(2):
                    pool.dma_start(hst[:, d, :], st0[l, d]).then_inc(state_in, 16)
                for k in range(2):
                    pool.wait_ge(st_done, count(l, 4, 2 + k))
                    pool.dma_start(news[l, k], eb[:, k, :]).then_inc(st_out, 16)
                for j in range(KT):
                    pool.wait_ge(gb_done, count(l, 24, KT + j))
                    nc.gpsimd.tensor_tensor(gates[:, j, :], gates[:, j, :], gates[:, KT + j, :], ALU.add).then_inc(mg_done, 1)
                sum_squares(l, False, KT * (2 * l + 1))
                if l + 1 < DEPTH:
                    pool.wait_ge(h_full, count(l, NFULL, NFULL - 1))
                    load_params(l + 1)
                for j in range(KT):
                    pool.wait_ge(sq_done, KT * (2 * l + 2) + j + 1)
                    if j == 0:
                        pool.wait_ge(misc_done, count(l, NMISC, M_N2))
                        nc.gpsimd.tensor_copy(sqa[:, :], th[:, 0, :]).then_inc(sq_sum, 1)
                    else:
                        pool.wait_ge(sq_sum, KT * (2 * l + 2) + j)
                        nc.gpsimd.tensor_tensor(sqa[:, :], sqa[:, :], th[:, j % 2, :], ALU.add).then_inc(sq_sum, 1)
            for j in range(KT):
                pool.wait_ge(y_ready, j + 1)
                pool.dma_start(y[:, j, :], gates[:, j, :]).then_inc(y_out, 16)
            pool.wait_ge(y_out, 16 * KT)
            pool.wait_ge(st_out, 32 * DEPTH)
            pool.wait_ge(k_out, 16 * DEPTH)
            pool.wait_ge(v_out, 16 * DEPTH)

        @block.tensor
        def _(pe):
            mm = nc.tensor.matmul

            def modulation(l, m):
                pe.wait_ge(mod_in[m % NMOD], mod_value(l, m))
                if m == MOD_HEAD:
                    pe.wait_ge(mod_read, count(l, 2, 0))
                for k in range(KT):
                    last = mm(modp[:, 2 * m:2 * m + 2], rawm[:, m % NMOD, P * k:P * k + P],
                              cs[:, 2 * k:2 * k + 2], start=(k == 0), stop=(k == KT - 1))
                last.then_inc(mod_used, 1)

            def misc_turn(l, i):
                if i:
                    misc_read(pe, l, i - 1)
                elif l:
                    misc_read(pe, l - 1, NMISC - 1)

            def three(out, sh, sl, mhi, mlo, start, stop):
                mm(out, sh, mhi, start=start, stop=False)
                mm(out, sh, mlo, start=False, stop=False)
                return mm(out, sl, mhi, start=False, stop=stop)

            def unit(l, u):
                kind, j, part = UNITS[u]
                s = u % NHL
                pe.wait_ge(lo_done, count(l, NU, u))

                def blk(b):
                    return wh[:, s, P * b:P * b + P], wl[:, s, P * b:P * b + P]

                def open_bank(g):
                    if g >= BANKS:
                        group_read(pe, l, g - BANKS)
                    return acc[g % BANKS]

                if kind == VV:
                    for kk in range(2):
                        k = 2 * part + kk
                        for c in range(NCH):
                            g = G_OF[(VV, c)]
                            bank = open_bank(g) if k == 0 else acc[g % BANKS]
                            tok = slice(CHUNK0[c], CHUNK0[c] + P)
                            wsl = slice(4 * P * kk, 4 * P * kk + 4 * P)
                            last = three(bank[:, :], hh[:, k, tok], hl[:, k, tok], wh[:, s, wsl], wl[:, s, wsl],
                                         k == 0, k == KT - 1)
                elif kind == BRANCH:
                    b = j // KT
                    src = ((hh, hl, 0), (hh, hl, 4), (osh, osl, 0))[b]
                    for jj in range(2):
                        g = G_OF[(BRANCH, j + jj)]
                        bank = open_bank(g)
                        for k in range(4):
                            if jj == 0 and j % KT == 0:
                                pe.wait_ge(h_lo, count(l, NSPLIT, (SP_OP, SP_OT, SP_Z)[b] + k))
                            w1, w2 = blk(4 * jj + k)
                            last = three(bank[:, 0:T], w1, w2, src[0][:, src[2] + k, :], src[1][:, src[2] + k, :],
                                         k == 0, k == 3)
                elif kind == DOWN:
                    g = G_OF[(DOWN, j)]
                    k0, k1 = DOWN_CUTS[part]
                    bank = open_bank(g) if part == 0 else acc[g % BANKS]
                    for k in range(k0, k1):
                        if j == 0:
                            pe.wait_ge(h_lo, count(l, NSPLIT, SP_FF + k))
                        w1, w2 = blk(k - k0)
                        last = three(bank[:, 0:T], w1, w2, ah[:, k, :], al[:, k, :], k == 0, k == FT - 1)
                else:
                    g = G_OF[(kind, j)]
                    bank = open_bank(g)
                    first = {XBC: SP_N1, OUT: SP_MG, UP: SP_N2}.get(kind) if j == 0 else None
                    srch, srcl = (mh, ml) if kind == OUT else (hh, hl)
                    for k in range(KT):
                        if first is not None:
                            pe.wait_ge(h_lo, count(l, NSPLIT, first + k))
                        w1, w2 = blk(k)
                        last = three(bank[:, 0:T], w1, w2, srch[:, k, :], srcl[:, k, :], k == 0, k == KT - 1)
                last.then_inc(unit_used, 1)

            def time_steps(l):
                misc_turn(l, M_DT)
                pe.wait_ge(par_ready, l + 1)
                for c in range(NCH):
                    tok = slice(CHUNK0[c], CHUNK0[c] + P)
                    for k in range(KT):
                        ws = slice(16 * k, 16 * k + 16)
                        last = three(mz[:, 16 * c:16 * c + 16], hh[:, k, tok], hl[:, k, tok], wdh[:, ws], wdl[:, ws],
                                     k == 0, k == KT - 1)
                last.then_inc(misc_done, 1)

            def cumulative(l):
                misc_turn(l, M_SM)
                pe.wait_ge(adt_done, l + 1)
                a3 = adt[:, :].rearrange("p (c h) -> p c h", c=NCH)
                n = NCH * SSD_H
                for i, (m_, d) in enumerate(((le, 0), (ge, 1), (gt, 0), (lt, 1))):
                    mm(mz[:, n * i:n * i + n], m_, a3[:, :, SSD_H * d:SSD_H * d + SSD_H], start=True, stop=True)
                mm(mz[:, 4 * n:6 * n], ones, adt[:, :], start=True, stop=True).then_inc(misc_done, 1)

            def scores(l, i):
                h, t = divmod(i, NCH)
                nk, k0 = (PAST + LAT, 0) if t < 2 else (SEQ, PAST + CTX0)
                if i == 0:
                    pe.wait_ge(qk_done, count(l, 2 * HEADS, 2 * HEADS - 1))
                    pe.wait_ge(cache_in, 32 * (l + 1))
                if i:
                    pe.wait_ge(exp_done, count(l, NATT, i - 1))
                for m_, bank in enumerate((mix5, mix6)):
                    q = slice(QK * m_, QK * m_ + QK)
                    last = mm(bank[:, 0:nk], qt[q, h, CHUNK0[t]:CHUNK0[t] + P], kt_[q, h, k0:k0 + nk],
                              start=True, stop=True)
                last.then_inc(s_done, 1)

            def transposes(l, i):
                n = 3 if i % NCH < 2 else 1
                pe.wait_ge(a_done, count(l, NATT, i))
                if i:
                    pe.wait_ge(at_done, count(l, NATT, i - 1))
                else:
                    pe.wait_ge(mod_read, count(l, 2, 1))
                for b in range(n):
                    last = nc.tensor.transpose(mix7[:, P * b:P * b + P], pr[:, i % 2, 0, P * b:P * b + P], ident)
                last.then_inc(tr_done, 1)

            def values(l, i):
                h, t = divmod(i, NCH)
                if i == 0:
                    pe.wait_ge(v_in, count(l, NCH, NCH - 1))
                pe.wait_ge(at_done, count(l, NATT, i))
                pe.wait_ge(exp_done, count(l, NATT, min(i + 1, NATT - 1)))
                if i:
                    pe.wait_ge(o_done, count(l, NATT, i - 1))
                tiles = (0, 1, 2) if t < 2 else (3,)
                for b, v in enumerate(tiles):
                    last = mm(mix5[:, 3 * P:4 * P], vv[:, v, P * h:P * h + P], at_[:, i % 2, P * b:P * b + P],
                              start=(b == 0), stop=(b == len(tiles) - 1))
                last.then_inc(av_done, 1)

            def chunk(l, c):
                tok = slice(CHUNK0[c], CHUNK0[c] + P)
                pe.wait_ge(cv_out, count(l, 8 + FT, 7))
                if c:
                    pe.wait_ge(xt_in, count(l, NCH, c - 1))
                else:
                    pe.wait_ge(o_done, count(l, NATT, NATT - 1))
                for j in range(4):
                    nc.tensor.transpose(mix5[:, P * j:P * j + P], xbc[:, j, tok], ident)
                for g in range(2):
                    nc.tensor.transpose(mix6[:, P * g:P * g + P], xbc[:, 4 + g, tok], ident)
                for g in range(2):
                    last = mm(mix6[:, P * (2 + g):P * (3 + g)], xbc[:, 4 + g, tok], xbc[:, 6 + g, tok],
                              start=True, stop=True)
                last.then_inc(xt_done, 1)

            def chunk_state(l, k):
                c, d = S_TASKS[k]
                pe.wait_ge(xw_done, count(l, 4, k))
                if k:
                    pe.wait_ge(st_done, count(l, 4, k - 1))
                else:
                    pe.wait_ge(at_done, count(l, NATT, NATT - 1))
                for g in range(2):
                    last = mm(mix7[:, 2 * P * g:2 * P * g + 2 * P], bg[:, c, P * g:P * g + P],
                              xw[:, 2 * P * g:2 * P * g + 2 * P], start=True, stop=True)
                last.then_inc(cst_done, 1)

            def rows(l, y_):
                c, g = divmod(y_, 2)
                if y_:
                    pe.wait_ge(d_done, count(l, NY, y_ - 1))
                    pe.wait_ge(e_done, count(l, NY, y_ - 1))
                else:
                    pe.wait_ge(xt_in, count(l, NCH, NCH - 1))
                for d, bank in enumerate((mix5, mix6)):
                    for i in range(4):
                        col = 16 * c + SSD_H * d + 4 * g + i
                        last = mm(bank[:, P * i:P * i + P], adt[:, col:col + 1].to_broadcast([P, P]), tri[d],
                                  start=True, stop=True)
                last.then_inc(bc_done, 1)

            def scan_out(l, y_):
                c, g = divmod(y_, 2)
                pe.wait_ge(m_done, count(l, NY, y_))
                if y_:
                    pe.wait_ge(yz_done, count(l, NY, y_ - 1))
                else:
                    pe.wait_ge(st_done, count(l, 4, 3))
                    pe.wait_ge(state_in, 32 * (l + 1))
                for i in range(4):
                    h = 4 * g + i
                    out = mix7[64 * (i % 2):64 * (i % 2) + 64, P * (i // 2):P * (i // 2) + P]
                    hs = slice(SSD_P * h, SSD_P * h + SSD_P)
                    ms = slice(P * i, P * i + P)
                    terms = [(xt[:, c, hs], ee[:, d, ms]) for d in range(2)]
                    if c < 2:
                        terms += [(hst[:, (0, 3)[d] if c == 0 else (2, 1)[d], hs], eb[:, d, ms]) for d in range(2)]
                    for n, (s_, m_) in enumerate(terms):
                        last = mm(out, s_, m_, start=(n == 0), stop=(n == len(terms) - 1))
                last.then_inc(y_done, 1)

            def mixers(l, s):
                if 2 <= s < NATT + 2:
                    values(l, s - 2)
                if 1 <= s < NATT + 1:
                    transposes(l, s - 1)
                if s < NATT:
                    scores(l, s)
                if s == 0:
                    time_steps(l)
                if s == 2:
                    cumulative(l)
                if SLOT_PW <= s < SLOT_PW + 4:
                    j = s - SLOT_PW
                    misc_turn(l, M_PW + j)
                    pe.wait_ge(pooled, count(l, 4, j))
                    mm(mz, prm_("plw", P * j, P), gates[:, 16 + j, :], start=True, stop=True).then_inc(misc_done, 1)
                if SLOT_X <= s < SLOT_X + NCH:
                    if s == SLOT_X:
                        pe.wait_ge(exp_done, count(l, NATT, NATT - 1))
                    chunk(l, s - SLOT_X)
                if SLOT_X <= s < SLOT_X + HEADS:
                    h = s - SLOT_X
                    misc_turn(l, M_ATT + h)
                    pe.wait_ge(osq_done, l + 1)
                    mm(mz, ones, rst[:, h, :], start=True, stop=True).then_inc(misc_done, 1)
                if SLOT_S <= s < SLOT_S + 4:
                    chunk_state(l, s - SLOT_S)
                if SLOT_Y + 1 <= s < SLOT_Y + NY + 1:
                    scan_out(l, s - SLOT_Y - 1)
                if SLOT_Y <= s < SLOT_Y + NY:
                    rows(l, s - SLOT_Y)
                if SLOT_RMS <= s < SLOT_RMS + 2:
                    g = s - SLOT_RMS
                    misc_turn(l, M_SSD + g)
                    pe.wait_ge(zsq_done, l + 1)
                    mm(mz, ones, rst[:, 2 * g, :], start=True, stop=False)
                    mm(mz, ones, rst[:, 2 * g + 1, :], start=False, stop=True).then_inc(misc_done, 1)

            pe.wait_ge(tab_in, 80)
            pe.wait_ge(cs_ready, 1)
            for l in range(DEPTH):
                misc_turn(l, 0)
                pe.wait_ge(sq_sum, KT * (2 * l + 1))
                mm(mz, ones, sqa[:, :], start=True, stop=True).then_inc(misc_done, 1)
                for m in range(MOD_HEAD):
                    modulation(l, m)
                for u in range(NU):
                    if UNITS[u] == (UP, 0, 0):
                        misc_turn(l, M_N2)
                        pe.wait_ge(sq_sum, KT * (2 * l + 2))
                        mm(mz, ones, sqa[:, :], start=True, stop=True).then_inc(misc_done, 1)
                    unit(l, u)
                    for m in mod_after(u):
                        modulation(l, m)
                    if MIX0 <= u <= MIX0 + SLOT_RMS + 1:
                        mixers(l, u - MIX0)
            misc_turn(DEPTH, 0)
            pe.wait_ge(sq_sum, KT * (2 * DEPTH + 1))
            mm(mz, ones, sqa[:, :], start=True, stop=True).then_inc(misc_done, 1)

        @block.scalar
        def _(act):
            af = nc.scalar.activation
            step = Steps(act, act_step)
            eps = tab_("eps")

            def hi(l, u):
                act.wait_ge(raw_in[raw_slot(u)], raw_value(l, u))
                if u >= NHL:
                    act.wait_ge(unit_used, count(l, NU, u - NHL))
                elif l:
                    act.wait_ge(unit_used, count(l - 1, NU, NU - 1))
                s, n = u % NHL, COLS[u]
                af(wh[:, s, 0:n], raw[:, raw_slot(u), 0:n], ACT.Copy).then_inc(hi_done, 1)

            def inv_rms(l, i, n):
                act.wait_ge(misc_done, count(l, NMISC, i))
                if i:
                    act.wait_ge(h_full, count(l, NFULL, F_N1 + KT - 1))
                elif l:
                    act.wait_ge(h_full, count(l - 1, NFULL, F_N2 + KT - 1))
                step.then(af(rs[:, :], mz, ACT.Ln, bias=eps, scale=1.0 / n))
                af(rs[:, :], rs[:, :], ACT.Exp, scale=-0.5).then_inc(rs_ready, 1)

            def high(l, full, dst, src):
                if full is not None:
                    act.wait_ge(h_full, count(l, NFULL, full))
                af(dst, src, ACT.Copy).then_inc(h_hi, 1)

            def square(first, j, after):
                if after is not None:
                    act.wait_ge(x_new, after + 1)
                if j >= 2:
                    act.wait_ge(sq_sum, first + j - 1)
                af(th[:, j % 2, :], x[:, j, :], ACT.Square).then_inc(sq_done, 1)

            def evac(l, g):
                kind, j = GROUPS[g]
                bank = acc[g % BANKS]
                group_done(act, l, g)
                if kind in (XBC, UP):
                    n = j if kind == XBC else 8 + j
                    w, b = ("cw", "cb") if kind == XBC else ("fw", "fb")
                    b_ = j % 2
                    tile = j if kind == XBC else (j // 2 + FT * (j % 2))
                    if kind == XBC and j < 2 or kind == UP and j < 2:
                        act.wait_ge(h_lo, count(l, NSPLIT, (SP_N1 if kind == XBC else SP_N2) + KT - 1))
                    elif kind == UP and b_ == 1:
                        act.wait_ge(h_lo, count(l, NSPLIT, SP_FF + j // 2 - 1))
                    else:
                        act.wait_ge(cv_out, count(l, 8 + FT, j - 2 if kind == XBC else 8 + j // 2 - 1))
                    af(cv[:, b_, :], bank[:, 0:T], ACT.Identity, bias=prm_(b, tile), scale=prm_(w, 3 * tile + 1)) \
                        .then_inc(cv_init, 1)
                elif kind == UU:
                    act.wait_ge(pads, l + 1)
                    af(ut[:, j, ULAT:ULAT + LAT], bank[:, 0:LAT], ACT.Copy)
                    af(ut[:, j, UCTX:UCTX + SEQ], bank[:, CTX0:T], ACT.Copy).then_inc(u_in, 1)
                elif kind in (QQ, KK):
                    dst = qt[:, j, :] if kind == QQ else kt_[:, j, PAST:PAST + T]
                    af(dst, bank[:, 0:T], ACT.Copy).then_inc(qk_in, 1)
                elif kind == VV:
                    af(vv[:, 1 + j, :], bank[:, :], ACT.Copy).then_inc(v_in, 1)
                elif kind == ZZ:
                    if j < 2:
                        act.wait_ge(qk_done, count(l, 2 * HEADS, 2 * HEADS - 1))
                    else:
                        act.wait_ge(z_done, count(l, 4, j - 2))
                    af(th[:, j % 2, :], bank[:, 0:T], ACT.Tanh, scale=0.5).then_inc(z_tanh, 1)
                elif kind == GATE:
                    if j >= 16:
                        act.wait_ge(op_done, count(l, 4, 3))
                    af(gates[:, j, :], bank[:, 0:T], ACT.Tanh, bias=bgh[:, j:j + 1], scale=0.5).then_inc(g_done, 1)

            def conv_silu(l, g):
                kind, j = GROUPS[g]
                n = j if kind == XBC else 8 + j
                if kind == XBC or kind == UP and j % 2 == 0:
                    act.wait_ge(cv_done, count(l, NCONV, n))
                    b_ = j % 2
                    if kind == UP and j:
                        act.wait_ge(h_full, count(l, NFULL, F_FF + j // 2 - 1))
                    af(th[:, b_, :], cv[:, b_, :], ACT.Tanh).then_inc(cv_tanh, 1)

            def probabilities(l, i):
                nk = PAST + LAT if i % NCH < 2 else SEQ
                act.wait_ge(nm_done, count(l, NATT, i))
                if i >= 2:
                    act.wait_ge(tr_done, count(l, NATT, i - 2))
                    act.wait_ge(a_done, count(l, NATT, i - 2))
                for m_, bank in enumerate((mix5, mix6)):
                    last = af(pr[:, i % 2, m_, 0:nk], bank[:, 0:nk], ACT.Exp, bias=nmb[:, i % 2, m_:m_ + 1],
                              scale=SCALE, accum_out=rsm[:, i % 2, m_:m_ + 1])
                last.then_inc(exp_done, 1)

            def mixers(l, s):
                if 2 <= s < NATT + 2:
                    i = s - 2
                    h, t = divmod(i, NCH)
                    act.wait_ge(av_done, count(l, NATT, i))
                    if s < NATT:
                        act.wait_ge(nm_done, count(l, NATT, s))
                    af(ot[:, h, CHUNK0[t]:CHUNK0[t] + P], mix5[:, 3 * P:4 * P], ACT.Copy).then_inc(o_done, 1)
                if 1 <= s < NATT + 1:
                    i = s - 1
                    n = P * (3 if i % NCH < 2 else 1)
                    act.wait_ge(tr_done, count(l, NATT, i))
                    if i >= 2:
                        act.wait_ge(av_done, count(l, NATT, i - 2))
                    af(at_[:, i % 2, 0:n], mix7[:, 0:n], ACT.Copy).then_inc(at_done, 1)
                if s < NATT:
                    probabilities(l, s)
                if s == 1:
                    act.wait_ge(dt_raw, l + 1)
                    step.then(af(dte[:, :], dte[:, :], ACT.Exp))
                    af(dte[:, :], dte[:, :], ACT.Ln, bias=1.0).then_inc(dt_log, 1)
                if s == 2:
                    act.wait_ge(sm_done, l + 1)
                    af(ede[:, :], sm[:, 48:144], ACT.Exp).then_inc(ede_done, 1)
                if s == SLOT_X:
                    act.wait_ge(o_done, count(l, NATT, NATT - 1))
                    act.wait_ge(a_done, count(l, NATT, NATT - 1))
                    act.wait_ge(av_done, count(l, NATT, NATT - 1))
                    act.wait_ge(k_out, 16 * (l + 1))
                    act.wait_ge(v_out, 16 * (l + 1))
                    af(rst[:, :, :], ot[:, :, :], ACT.Square).then_inc(osq_done, 1)
                if SLOT_X <= s < SLOT_X + NCH:
                    c = s - SLOT_X
                    act.wait_ge(xt_done, count(l, NCH, c))
                    af(xt[:, c, :], mix5[:, :], ACT.Copy)
                    af(bg[:, c, :], mix6[:, :], ACT.Copy).then_inc(xt_in, 1)
                if SLOT_X <= s < SLOT_X + HEADS:
                    h = s - SLOT_X
                    act.wait_ge(misc_done, count(l, NMISC, M_ATT + h))
                    af(rst[:, h, :], mz, ACT.Copy).then_inc(att_ss, 1)
                    if h == HEADS - 1:
                        act.wait_ge(att_ss, count(l, HEADS, h))
                        step.then(af(rst[:, :, :], rst[:, :, :], ACT.Ln, bias=eps, scale=1.0 / P))
                        af(rst[:, :, :], rst[:, :, :], ACT.Exp, scale=-0.5).then_inc(ors_done, 1)
                if SLOT_S + 2 <= s < SLOT_S + 4:
                    k = s - SLOT_S
                    act.wait_ge(cst_done, count(l, 4, k))
                    act.wait_ge(on_done, l + 1)
                    if l and k == 2:
                        act.wait_ge(st_out, 32 * l)
                    af(eb[:, k - 2, :], mix7[:, :], ACT.Copy).then_inc(st_done, 1)
                if SLOT_Y <= s < SLOT_Y + NY:
                    y_ = s - SLOT_Y
                    act.wait_ge(bc_done, count(l, NY, y_))
                    if y_ == 0:
                        act.wait_ge(st_out, 32 * (l + 1))
                    act.wait_ge(d_done, count(l, NY, y_))
                    if y_ // 2 < 2:
                        if y_:
                            act.wait_ge(y_done, count(l, NY, y_ - 1))
                        for d, bank in enumerate((mix5, mix6)):
                            af(eb[:, d, :], bank[:, :], ACT.Exp)
                    af(ee[:, :, :], ee[:, :, :], ACT.Exp).then_inc(e_done, 1)
                if s == SLOT_RMS:
                    act.wait_ge(yz_done, count(l, NY, NY - 1))
                    act.wait_ge(y_done, count(l, NY, NY - 1))
                    af(rst[:, :, :], zz[:, :, :], ACT.Square).then_inc(zsq_done, 1)
                if SLOT_RMS <= s < SLOT_RMS + 2:
                    g = s - SLOT_RMS
                    act.wait_ge(misc_done, count(l, NMISC, M_SSD + g))
                    af(rst[:, 2 * g, :], mz, ACT.Copy).then_inc(z_ss, 1)
                    if g == 1:
                        act.wait_ge(z_ss, count(l, 2, g))
                        for g_ in range(2):
                            step.then(af(rst[:, 2 * g_, :], rst[:, 2 * g_, :], ACT.Ln, bias=eps, scale=0.5 / P))
                            last = af(rst[:, 2 * g_, :], rst[:, 2 * g_, :], ACT.Exp, scale=-0.5)
                        last.then_inc(zrs_done, 1)

            act.wait_ge(cs_half, 1)
            af(cst[:, :], csh[:, :], ACT.Tanh).then_inc(cs_tanh, 1)
            act.wait_ge(tab_in, 80)
            act.wait_ge(zeroed, 2)
            for j in range(KT):
                square(0, j, None)
            for l in range(DEPTH):
                act.wait_ge(par_in, 16 * (l + 1))
                if l:
                    act.wait_ge(wdc_done, l)
                af(eal[:, :], prm_("alog", 0, 16), ACT.Exp)
                af(wdh[:, :], prm_("wdt", 0, KT * 16), ACT.Copy).then_inc(wd_hi, 1)
                act.wait_ge(lam_sum, l + 1)
                af(lams[:, 2:4], lams[:, 0:2], ACT.Exp).then_inc(lam_exp, 1)
                for u in range(AHEAD):
                    hi(l, u)
                inv_rms(l, 0, D)
                for j in range(KT):
                    high(l, F_N1 + j, hh[:, j, :], cv[:, j % 2, :])
                for u in range(NU):
                    if UNITS[u] == (UP, 0, 0):
                        inv_rms(l, M_N2, D)
                        for j in range(KT):
                            high(l, F_N2 + j, hh[:, j, :], cv[:, j % 2, :])
                    done = done_after(u)
                    for g in done:
                        if GROUPS[g][0] in (XBC, UU, QQ, KK, VV, ZZ, GATE, UP):
                            evac(l, g)
                    if u + AHEAD < NU:
                        hi(l, u + AHEAD)
                    for g in done:
                        kind, j = GROUPS[g]
                        if kind in (XBC, UP):
                            conv_silu(l, g)
                            if kind == UP and j % 2:
                                high(l, F_FF + j // 2, ah[:, j // 2, :], cv[:, 1, :])
                        if kind in (OUT, DOWN):
                            first = KT * (2 * l + (kind == DOWN))
                            square(KT + first, j, first + j)
                        if kind == BRANCH and j >= 2 * KT:
                            high(l, F_MG + j - 2 * KT, mh[:, j - 2 * KT, :], cv[:, j % 2, :])
                    if MIX0 <= u <= MIX0 + SLOT_RMS + 1:
                        s = u - MIX0
                        mixers(l, s)
                        if s == SLOT_Y + NY:
                            group_done(act, l, G_OF[(GATE, 23)])
                            act.wait_ge(op_done, count(l, 4, 3))
                            act.wait_ge(on_done, l + 1)
                            for i in range(4):
                                high(l, None, hh[:, i, :], ut[:, i, 0:T])
                            for i in range(4):
                                high(l, None, hh[:, 4 + i, :], ot[:, i, :])
                        if s == SLOT_RMS + 1:
                            for i in range(4):
                                act.wait_ge(zn_done, count(l, 4, i))
                                high(l, None, osh[:, i, :], zz[:, i, :])
            inv_rms(DEPTH, 0, D)

        @block.vector
        def _(dve):
            ts, tt, stt = nc.vector.tensor_scalar, nc.vector.tensor_tensor, nc.vector.scalar_tensor_tensor
            step = Steps(dve, dve_step)

            def lo(l, u):
                dve.wait_ge(hi_done, count(l, NU, u))
                s, n = u % NHL, COLS[u]
                tt(wl[:, s, 0:n], raw[:, raw_slot(u), 0:n], wh[:, s, 0:n].bitcast(F32), ALU.subtract).then_inc(lo_done, 1)

            def low(l, i, dst, src, high_):
                dve.wait_ge(h_hi, count(l, NSPLIT, i))
                tt(dst, src, high_.bitcast(F32), ALU.subtract).then_inc(h_lo, 1)

            def norm(l, nth, split0, scale, shift0):
                dve.wait_ge(rs_ready, 2 * l + nth + 1)
                for j in range(KT):
                    b = cv[:, j % 2, :]
                    if j >= 2:
                        dve.wait_ge(h_lo, count(l, NSPLIT, split0 + j - 2))
                    step.then(tt(b, x[:, j, :], rs[:, :], ALU.mult))
                    for v, (a0, a1) in enumerate(SEGS):
                        last = ts(b[:, a0:a1], b[:, a0:a1], scale[:, j, v:v + 1], mod[:, shift0 + j, v:v + 1],
                                  ALU.mult, ALU.add)
                    last.then_inc(h_full, 1)
                    if j:
                        low(l, split0 + j - 1, hl[:, j - 1, :], cv[:, (j - 1) % 2, :], hh[:, j - 1, :])
                low(l, split0 + KT - 1, hl[:, KT - 1, :], cv[:, (KT - 1) % 2, :], hh[:, KT - 1, :])

            def modulation(l, t0, t1):
                dve.wait_ge(mod_used, count(l, MODT, t1 - 1))
                tt(mod[:, t0:t1, :], modp[:, 2 * t0:2 * t1].rearrange("p (t v) -> p t v", v=2),
                   prm_("bmod", t0, t1 - t0).unsqueeze(2).to_broadcast([P, t1 - t0, 2]), ALU.add).then_inc(mod_read, 1)
                dve.wait_ge(mod_read, count(l, 2, t0 > 0))

            def scale_of(dst, t0, g):
                step.then(ts(dst[:, :, :], mod[:, t0:t0 + KT, :], 1.0, None, ALU.add))
                step.then(tt(dst[:, :, :], dst[:, :, :], prm_(g, 0, KT).unsqueeze(2).to_broadcast([P, KT, 2]), ALU.mult))

            def params(l):
                dve.wait_ge(par_in, 16 * (l + 1))
                lp = prm_("lam", 0, 4 * QK).rearrange("p (a b d) -> p a b d", a=2, b=2)
                step.then(tt(lamt[:, :, :], lp[:, :, 0, :], lp[:, :, 1, :], ALU.mult))
                nc.vector.reduce_sum(lams[:, 0:2], lamt[:, :, :], AX.X).then_inc(lam_sum, 1)
                ts(prm_("cw", 0, 32), prm_("cw", 0, 32), 0.5, None, ALU.mult)
                ts(prm_("fw", 0, 3 * FT), prm_("fw", 0, 3 * FT), 0.5, None, ALU.mult)
                ts(prm_("fb", 0, FT), prm_("fb", 0, FT), 0.5, None, ALU.mult)
                ts(bgh[:, :], prm_("bgate", 0, 24), 0.5, None, ALU.mult)
                step.then(tt(sg[:, :], prm_("subg"), prm_("oml"), ALU.mult))
                dve.wait_ge(wd_hi, l + 1)
                tt(wdl[:, :], prm_("wdt", 0, KT * 16), wdh[:, :].bitcast(F32), ALU.subtract)
                dve.wait_ge(lam_exp, l + 1)
                stt(out=nlam[:, :], in0=lams[:, 3:4], scalar=lams[:, 2:3], in1=prm_("li"), op0=ALU.subtract,
                    op1=ALU.subtract).then_inc(par_ready, 1)
                dve.wait_ge(par_ready, l + 1)

            def taps(l, g):
                kind, j = GROUPS[g]
                n = j if kind == XBC else 8 + j
                w = "cw" if kind == XBC else "fw"
                tile = j if kind == XBC else (j // 2 + FT * (j % 2))
                b = cv[:, j % 2, :]
                bank = acc[g % BANKS]
                dve.wait_ge(cv_init, count(l, NCONV, n))
                step.then(stt(out=b[:, 1:T], in0=bank[:, 0:T - 1], scalar=prm_(w, 3 * tile), in1=b[:, 1:T],
                              op0=ALU.mult, op1=ALU.add))
                stt(out=b[:, 0:T - 1], in0=bank[:, 1:T], scalar=prm_(w, 3 * tile + 2), in1=b[:, 0:T - 1],
                    op0=ALU.mult, op1=ALU.add).then_inc(cv_done, 1)

            def conv_result(l, g):
                kind, j = GROUPS[g]
                if kind == XBC:
                    dve.wait_ge(cv_tanh, count(l, 8 + FT, j))
                    stt(out=xbc[:, j, :], in0=th[:, j % 2, :], scalar=1.0, in1=cv[:, j % 2, :], op0=ALU.add,
                        op1=ALU.mult).then_inc(cv_out, 1)
                elif j % 2 == 0:
                    dve.wait_ge(cv_tanh, count(l, 8 + FT, 8 + j // 2))
                    stt(out=th[:, 0, :], in0=th[:, 0, :], scalar=1.0, in1=cv[:, 0, :], op0=ALU.add,
                        op1=ALU.mult).then_inc(cv_out, 1)
                else:
                    dve.wait_ge(cv_out, count(l, 8 + FT, 8 + j // 2))
                    dve.wait_ge(cv_done, count(l, NCONV, 8 + j))
                    tt(cv[:, 1, :], th[:, 0, :], cv[:, 1, :], ALU.mult).then_inc(h_full, 1)

            def rotate(l, g):
                kind, j = GROUPS[g]
                i = j if kind == QQ else HEADS + j
                dst = qt[:, j, 0:LAT] if kind == QQ else kt_[:, j, PAST:PAST + LAT]
                dve.wait_ge(qk_in, count(l, 2 * HEADS, i))
                swap = [(k + 16) % 32 for k in range(32)]
                step.then(nc.vector.stream_shuffle(th[:, i % 2, 0:LAT], dst, swap))
                tt(dst, dst, cos, ALU.mult)
                step.then(tt(th[:, i % 2, 0:LAT], th[:, i % 2, 0:LAT], sin, ALU.mult))
                tt(dst, dst, th[:, i % 2, 0:LAT], ALU.add).then_inc(qk_done, 1)

            def branch(l, g):
                kind, j = GROUPS[g]
                b, jj = divmod(j, KT)
                group_done(dve, l, g)
                if j == 0:
                    dve.wait_ge(g_done, count(l, 24, 23))
                stt(out=gates[:, j, :], in0=gates[:, j, :], scalar=1.0, in1=acc[g % BANKS][:, 0:T],
                    op0=ALU.add, op1=ALU.mult).then_inc(gb_done, 1)
                if b == 2:
                    dve.wait_ge(gb_done, count(l, 24, j))
                    dve.wait_ge(mg_done, count(l, KT, jj))
                    if jj >= 2:
                        dve.wait_ge(h_hi, count(l, NSPLIT, SP_MG + jj - 2))
                    tt(cv[:, j % 2, :], gates[:, jj, :], gates[:, j, :], ALU.add).then_inc(h_full, 1)
                    low_merged.append(jj)

            def update(l, g):
                kind, j = GROUPS[g]
                group_done(dve, l, g)
                for v, (a0, a1) in enumerate(SEGS):
                    gate = g1h[:, j, v:v + 1] if kind == OUT else mod[:, 5 * KT + j, v:v + 1]
                    last = stt(out=x[:, j, a0:a1], in0=acc[g % BANKS][:, a0:a1], scalar=gate, in1=x[:, j, a0:a1],
                               op0=ALU.mult, op1=ALU.add)
                last.then_inc(x_new, 1)

            def softmax_max(l, i):
                nk = PAST + LAT if i % NCH < 2 else SEQ
                dve.wait_ge(s_done, count(l, NATT, i))
                nc.vector.reduce_max(mxb[:, i % 2, 0:1], mix5[:, 0:nk], AX.X)
                step.then(nc.vector.reduce_max(mxb[:, i % 2, 1:2], mix6[:, 0:nk], AX.X))
                if i >= 2:
                    dve.wait_ge(exp_done, count(l, NATT, i - 2))
                ts(nmb[:, i % 2, :], mxb[:, i % 2, :], -SCALE, None, ALU.mult).then_inc(nm_done, 1)

            def softmax_mix(l, i):
                nk = PAST + LAT if i % NCH < 2 else SEQ
                dve.wait_ge(exp_done, count(l, NATT, i))
                step.then(nc.vector.reciprocal(rcp[:, 0:2], rsm[:, i % 2, :]))
                step.then(tt(rcp[:, 2:3], rcp[:, 1:2], nlam[:, :], ALU.mult))
                p0, p1 = pr[:, i % 2, 0, 0:nk], pr[:, i % 2, 1, 0:nk]
                step.then(ts(p1, p1, rcp[:, 2:3], None, ALU.mult))
                stt(out=p0, in0=p0, scalar=rcp[:, 0:1], in1=p1, op0=ALU.mult, op1=ALU.add).then_inc(a_done, 1)

            def weighted(l, k):
                c, d = S_TASKS[k]
                if k:
                    dve.wait_ge(cst_done, count(l, 4, k - 1))
                n = NCH * SSD_H
                w_ = wdc[:, n * d + SSD_H * c:n * d + SSD_H * c + SSD_H]
                tt(xw[:, :].rearrange("p (h q) -> p h q", h=SSD_H), xt[:, c, :].rearrange("p (h q) -> p h q", h=SSD_H),
                   w_.unsqueeze(2).to_broadcast([P, SSD_H, SSD_P]), ALU.mult).then_inc(xw_done, 1)

            def enter_state(l, k):
                c, d = S_TASKS[k]
                dve.wait_ge(cst_done, count(l, 4, k))
                dve.wait_ge(state_in, 32 * (l + 1))
                tot = ede[:, 48 + 16 * c + SSD_H * d:48 + 16 * c + SSD_H * d + SSD_H]
                step.then(tt(hst[:, 2 + k, :].rearrange("p (h q) -> p h q", h=SSD_H),
                             hst[:, d, :].rearrange("p (h q) -> p h q", h=SSD_H),
                             tot.unsqueeze(2).to_broadcast([P, SSD_H, SSD_P]), ALU.mult))
                tt(hst[:, 2 + k, :], hst[:, 2 + k, :], mix7[:, :], ALU.add).then_inc(st_done, 1)

            def decays(l, y_):
                c, g = divmod(y_, 2)
                dve.wait_ge(bc_done, count(l, NY, y_))
                if y_:
                    dve.wait_ge(y_done, count(l, NY, y_ - 1))
                else:
                    dve.wait_ge(on_done, l + 1)
                n = NCH * SSD_H
                for d, bank in enumerate((mix5, mix6)):
                    for i in range(4):
                        col = n * d + SSD_H * c + 4 * g + i
                        last = stt(out=ee[:, d, P * i:P * i + P], in0=bank[:, P * i:P * i + P], scalar=nac[:, col:col + 1],
                                   in1=neg[d], op0=ALU.add, op1=ALU.add)
                last.then_inc(d_done, 1)

            def matrices(l, y_):
                c, g = divmod(y_, 2)
                dve.wait_ge(e_done, count(l, NY, y_))
                for d in range(2):
                    for i in range(4):
                        col = 16 * c + SSD_H * d + 4 * g + i
                        m_ = ee[:, d, P * i:P * i + P]
                        last = stt(out=m_, in0=m_, scalar=dtt[:, col:col + 1], in1=bg[:, c, P * (2 + g):P * (3 + g)],
                                   op0=ALU.mult, op1=ALU.mult)
                    if c < 2:
                        e3 = eb[:, d, :].rearrange("p (i t) -> p i t", i=4)
                        last = tt(e3, e3, xbc[:, 6 + g, CHUNK0[c]:CHUNK0[c] + P].unsqueeze(1).to_broadcast([P, 4, P]),
                                  ALU.mult)
                last.then_inc(m_done, 1)

            def gate_z(l, y_):
                c, g = divmod(y_, 2)
                tok = slice(CHUNK0[c], CHUNK0[c] + P)
                dve.wait_ge(y_done, count(l, NY, y_))
                for i in range(2):
                    t_ = 2 * g + i
                    step.then(stt(out=cv[:, 0, P * i:P * i + P], in0=xbc[:, t_, tok], scalar=prm_("ssdD", t_),
                                  in1=mix7[:, P * i:P * i + P], op0=ALU.mult, op1=ALU.add))
                for i in range(2):
                    t_ = 2 * g + i
                    last = stt(out=zz[:, t_, tok], in0=cv[:, 0, P * i:P * i + P], scalar=0.5, in1=zz[:, t_, tok],
                               op0=ALU.mult, op1=ALU.mult)
                last.then_inc(yz_done, 1)

            def mixers_a(l, s):
                if s < NATT:
                    softmax_max(l, s)
                if s == 0:
                    dve.wait_ge(misc_done, count(l, NMISC, M_DT))
                    step.then(tt(dtv[:, :].rearrange("p (c h) -> p c h", c=NCH),
                                 mz[:, 0:48].rearrange("p (c h) -> p c h", c=NCH),
                                 prm_("dtb", 0, 16).unsqueeze(1).to_broadcast([P, NCH, 16]), ALU.add))
                    stt(out=dte[:, :], in0=dtv[:, :], scalar=-1.0, in1=dtv[:, :], op0=ALU.mult, op1=ALU.min) \
                        .then_inc(dt_raw, 1)
                if s == 1:
                    dve.wait_ge(dt_log, l + 1)
                    step.then(stt(out=dtt[:, :], in0=dtv[:, :], scalar=0.0, in1=dte[:, :], op0=ALU.max, op1=ALU.add))
                    stt(out=adt[:, :].rearrange("p (c h) -> p c h", c=NCH), in0=dtt[:, :].rearrange("p (c h) -> p c h", c=NCH),
                        scalar=-1.0, in1=eal[:, :].unsqueeze(1).to_broadcast([P, NCH, 16]), op0=ALU.mult,
                        op1=ALU.mult).then_inc(adt_done, 1)
                if s == 2:
                    dve.wait_ge(misc_done, count(l, NMISC, M_SM))
                    nc.vector.tensor_copy(sm[:, :], mz[:, 0:144]).then_inc(sm_done, 1)
                    dve.wait_ge(sm_done, l + 1)
                    ts(nac[:, :], sm[:, 0:48], -1.0, None, ALU.mult)
                    dve.wait_ge(ede_done, l + 1)
                    for d in range(2):
                        last = tt(wdc[:, 24 * d:24 * d + 24].rearrange("p (c h) -> p c h", c=NCH),
                                  dtt[:, :].rearrange("p (c h) -> p c h", c=NCH)[:, :, SSD_H * d:SSD_H * d + SSD_H],
                                  ede[:, 24 * d:24 * d + 24].rearrange("p (c h) -> p c h", c=NCH), ALU.mult)
                    last.then_inc(wdc_done, 1)
                if SLOT_PW <= s < SLOT_PW + 4:
                    j = s - SLOT_PW
                    dve.wait_ge(misc_done, count(l, NMISC, M_PW + j))
                    ts(ut[:, j, 0:T], mz, prm_("pscale", j), None, ALU.mult).then_inc(op_done, 1)
                if SLOT_Y + 1 <= s < SLOT_Y + NY + 1:
                    gate_z(l, s - SLOT_Y - 1)
                if SLOT_Y <= s < SLOT_Y + NY:
                    decays(l, s - SLOT_Y)

            def mixers_b(l, s):
                if s < NATT:
                    softmax_mix(l, s)
                if SLOT_S <= s < SLOT_S + 2:
                    enter_state(l, s - SLOT_S)
                if SLOT_S - 1 <= s < SLOT_S + 3:
                    if s == SLOT_S - 1:
                        dve.wait_ge(xt_in, count(l, NCH, NCH - 1))
                        dve.wait_ge(wdc_done, l + 1)
                    weighted(l, s - SLOT_S + 1)
                if s == SLOT_X + HEADS:
                    dve.wait_ge(ors_done, l + 1)
                    for h in range(HEADS):
                        last = stt(out=ot[:, h, :], in0=ot[:, h, :], scalar=sg[:, 0:1], in1=rst[:, h, :], op0=ALU.mult,
                                   op1=ALU.mult)
                    last.then_inc(on_done, 1)
                if SLOT_Y <= s < SLOT_Y + NY:
                    matrices(l, s - SLOT_Y)
                if s == SLOT_Y + NY:
                    for i in range(4):
                        low(l, SP_OP + i, hl[:, i, :], ut[:, i, 0:T], hh[:, i, :])
                    for i in range(4):
                        low(l, SP_OT + i, hl[:, 4 + i, :], ot[:, i, :], hh[:, 4 + i, :])
                if s == SLOT_RMS + 1:
                    dve.wait_ge(zrs_done, l + 1)
                    for i in range(4):
                        stt(out=zz[:, i, :], in0=zz[:, i, :], scalar=prm_("ssdg", i), in1=rst[:, 2 * (i // 2), :],
                            op0=ALU.mult, op1=ALU.mult).then_inc(zn_done, 1)
                    for i in range(4):
                        low(l, SP_Z + i, osl[:, i, :], zz[:, i, :], osh[:, i, :])

            low_merged = []
            dve.wait_ge(tab_in, 80)
            ts(csh[:, :], cs[:, :], 0.5, None, ALU.mult).then_inc(cs_half, 1)
            dve.wait_ge(cs_tanh, 1)
            stt(out=cs[:, :], in0=cst[:, :], scalar=1.0, in1=csh[:, :], op0=ALU.add, op1=ALU.mult).then_inc(cs_ready, 1)
            dve.wait_ge(zeroed, 2)
            for l in range(DEPTH):
                params(l)
                for u in range(AHEAD):
                    lo(l, u)
                modulation(l, 0, MOD_HEAD)
                scale_of(sc1, KT, "n1g")
                norm(l, 0, SP_N1, sc1, 0)
                for u in range(NU):
                    if UNITS[u] == (UP, 0, 0):
                        norm(l, 1, SP_N2, sc2, 3 * KT)
                    done = done_after(u)
                    for g in done:
                        if GROUPS[g][0] in (XBC, UP):
                            group_done(dve, l, g)
                            taps(l, g)
                        if GROUPS[g][0] == BRANCH:
                            branch(l, g)
                    if MIX0 <= u <= MIX0 + SLOT_RMS + 1:
                        mixers_a(l, u - MIX0)
                    if u + AHEAD < NU:
                        lo(l, u + AHEAD)
                    for g in done:
                        kind, j = GROUPS[g]
                        if kind in (XBC, UP):
                            conv_result(l, g)
                            if kind == UP and j % 2:
                                low(l, SP_FF + j // 2, al[:, j // 2, :], cv[:, 1, :], ah[:, j // 2, :])
                        if kind in (QQ, KK):
                            rotate(l, g)
                        if kind == ZZ:
                            dve.wait_ge(z_tanh, count(l, 4, j))
                            stt(out=zz[:, j, :], in0=th[:, j % 2, :], scalar=1.0, in1=acc[g % BANKS][:, 0:T],
                                op0=ALU.add, op1=ALU.mult).then_inc(z_done, 1)
                        if kind in (OUT, DOWN):
                            update(l, g)
                    while low_merged:
                        jj = low_merged.pop(0)
                        low(l, SP_MG + jj, ml[:, jj, :], cv[:, jj % 2, :], mh[:, jj, :])
                    if MIX0 <= u <= MIX0 + SLOT_RMS + 1:
                        mixers_b(l, u - MIX0)
                    if MODT - 1 in mod_after(u):
                        modulation(l, MOD_HEAD, MODT)
                        scale_of(sc2, 4 * KT, "n2g")
                        step.then(ts(g1h[:, :, :], mod[:, 2 * KT:3 * KT, :], 0.5, None, ALU.mult))
            dve.wait_ge(rs_ready, 2 * DEPTH + 1)
            for j in range(KT):
                stt(out=gates[:, j, :], in0=x[:, j, :], scalar=fg[:, j:j + 1], in1=rs[:, :], op0=ALU.mult,
                    op1=ALU.mult).then_inc(y_ready, 1)


def _tiles(a):
    return a.reshape(-1, P, a.shape[-1]).transpose(1, 0, 2)


def _stream(w_in, w_gate, w_branch, w_out, w_up, w_down, w_mod):
    c0 = {UU: 0, QQ: 512, KK: 1024, VV: 1536, ZZ: 2048, XBC: 2560}
    w_in, w_gate, w_branch, w_out, w_up, w_down, w_mod = (
        _tiles(w) for w in (w_in, w_gate, w_branch, w_out, w_up, w_down, w_mod))
    out = np.zeros((NS, P, KT * P), w_in.dtype)
    for i, (what, n) in enumerate(STREAM):
        if what == "mod":
            a = w_mod[:, :, P * n:P * n + P]
        else:
            kind, j, part = UNITS[n]
            col = slice(P * j, P * j + P)
            if kind == VV:
                a = w_in[:, 2 * part:2 * part + 2, c0[VV]:c0[VV] + 4 * P]
            elif kind in c0:
                a = w_in[:, :, c0[kind] + P * j:c0[kind] + P * j + P]
            elif kind == GATE:
                a = w_gate[:, :, col]
            elif kind == BRANCH:
                b, jj = divmod(j, KT)
                rows = w_branch[:, 4 * b:4 * b + 4, :]
                a = np.concatenate([rows[:, :, P * t:P * t + P] for t in (jj, jj + 1)], axis=1)
            elif kind == OUT:
                a = w_out[:, :, col]
            elif kind == UP:
                t = j // 2 + FT * (j % 2)
                a = w_up[:, :, P * t:P * t + P]
            else:
                a = w_down[:, DOWN_CUTS[part][0]:DOWN_CUTS[part][1], col]
        a = a.reshape(P, -1)
        out[i, :, :a.shape[1]] = a
    return out


def kernel(**inputs):
    import concourse.bacc as _bacc
    from concourse.bass_utils import run_bass_kernel_spmd as _run

    v = {k: np.ascontiguousarray(a) for k, a in inputs.items()}

    def per_channel(a):
        return a.reshape(-1, P).T

    def everywhere(a):
        return np.broadcast_to(a.reshape(1, -1), (P, a.size))

    par = np.zeros((DEPTH, P, NPAR), np.float32)
    for l in range(DEPTH):
        lam_init = 0.8 - 0.6 * float(np.exp(-0.3 * l))
        taps = {n: v[k][l].reshape(3, -1, P).transpose(2, 1, 0).reshape(P, -1)
                for n, k in (("cw", "ssd_conv_w"), ("fw", "ffn_conv_w"))}
        cols = {
            "bmod": per_channel(v["b_mod"][l]), "n1g": per_channel(v["norm1_g"][l]), "n2g": per_channel(v["norm2_g"][l]),
            "pscale": per_channel(v["pool_scale"][l]), "subg": per_channel(v["att_subln_g"][l]),
            "li": np.full((P, 1), lam_init), "oml": np.full((P, 1), 1.0 - lam_init),
            "cw": taps["cw"], "cb": per_channel(v["ssd_conv_b"][l]), "ssdg": per_channel(v["ssd_norm_g"][l]),
            "ssdD": per_channel(np.repeat(v["ssd_D"][l], SSD_P)), "bgate": per_channel(v["b_gate"][l]),
            "fw": taps["fw"], "fb": per_channel(v["ffn_conv_b"][l]), "dtb": everywhere(v["ssd_dt_bias"][l]),
            "alog": everywhere(v["ssd_A_log"][l]), "lam": everywhere(v["att_lambda"][l]),
            "wdt": _tiles(v["w_in"][l][:, 3584:3600]).reshape(P, -1),
            "plw": v["pool_w"][l].transpose(1, 0, 2).reshape(P, -1),
        }
        for name, a in cols.items():
            at, n = PAR[name]
            par[l, :, at:at + n] = a

    def token_tiles(a):
        return a.T.reshape(KT, P, -1).transpose(1, 0, 2)

    kcache = v["cache_attn_k"][0]
    ins = {
        "wstream": np.stack([_stream(*(v[k][l] for k in ("w_in", "w_gate", "w_branch", "w_out", "ffn_w_up", "ffn_w_down",
                                                         "w_mod"))) for l in range(DEPTH)]),
        "par": par,
        "tab": tables(),
        "xs": token_tiles(v["x_sample"][0]),
        "xp": token_tiles(v["x_prompt"][0]),
        "cvec": np.stack([per_channel(v["c"][0]), per_channel(v["c_ctx"])], axis=2).reshape(P, 2 * KT),
        "kc": kcache.transpose(0, 3, 4, 2, 1).reshape(DEPTH, P, HEADS, PAST),
        "vc": v["cache_attn_v"][0].reshape(DEPTH, PAST, 4 * P),
        "st0": v["state_ssd"][0].transpose(0, 1, 4, 2, 3).reshape(DEPTH, 2, P, 4 * P),
        "fng": per_channel(v["final_norm_g"]),
    }
    outs = {"y": (P, KT, T), "newk": (DEPTH, P, HEADS, SEQ), "newv": (DEPTH, P, 4 * P), "news": (DEPTH, 2, P, 4 * P)}
    nc = _bacc.Bacc("TRN2", target_bir_lowering=False, num_devices=1)
    arrays, args = {}, []
    for name, a in ins.items():
        a = np.ascontiguousarray(a, dtype=np.float32)
        arrays[f"in_{name}_dram"] = a
        args.append(nc.dram_tensor(f"in_{name}_dram", a.shape, F32, kind="ExternalInput").ap())
    for name, shape in outs.items():
        args.append(nc.dram_tensor(f"out_{name}_dram", shape, F32, kind="ExternalOutput").ap())
    build(nc, *args)
    res = _run(nc, [arrays], core_ids=[0]).results[0]
    yt = res["out_y_dram"].transpose(2, 1, 0).reshape(T, D)
    nk = res["out_newk_dram"].reshape(DEPTH, 2, QK, HEADS, SEQ).transpose(0, 4, 3, 1, 2)
    nv = res["out_newv_dram"].reshape(DEPTH, SEQ, HEADS, 2 * QK)
    ns = res["out_news_dram"].reshape(DEPTH, 2, P, SSD_H, SSD_P).transpose(0, 1, 3, 4, 2)
    return tuple(np.ascontiguousarray(a[None]) for a in (yt[CTX0:], yt[:LAT], nk, nv, ns))
```

```python
from contextlib import ExitStack

import numpy as np

import concourse.bass as bass
from concourse import mybir

F32 = mybir.dt.float32
F32R = mybir.dt.float32r
ALU = mybir.AluOpType
ACT = mybir.ActivationFunctionType
AX = mybir.AxisListType

P = 128
D = 1024
KT = D // P
DEPTH = 2
SEQ, LAT, PAST = 128, 256, 128
GRID_W = 64
EPS = 1e-6
GAP = 2
CTX0 = LAT + GAP
T = CTX0 + SEQ
SEGS = ((0, LAT), (CTX0, T))
CHUNK0 = (0, P, CTX0)
NCH = 3
HEADS = 4
QK = 64
SCALE = QK ** -0.5
SSD_H, SSD_P, SSD_G = 8, 64, 2
WINDOWS = (2, 4, 8, 16)
PADL = 8
ULAT, UCTX = PADL, PADL + LAT + 2 * PADL
UW = UCTX + SEQ + PADL
FFN = ((8 * D // 3 + 127) // 128) * 128
FT = FFN // P
NEG = -1e30

XBC, UU, QQ, KK, VV, ZZ, GATE, BRANCH, OUT, UP, DOWN = (
    "xbc", "u", "q", "k", "v", "z", "gate", "branch", "out", "up", "down")
GROUPS = ([(XBC, j) for j in range(8)] + [(UU, j) for j in range(4)] + [(QQ, j) for j in range(4)]
          + [(KK, j) for j in range(4)] + [(VV, c) for c in range(NCH)] + [(ZZ, j) for j in range(4)]
          + [(GATE, j) for j in range(24)] + [(BRANCH, j) for j in range(24)]
          + [(OUT, j) for j in range(8)] + [(UP, j) for j in range(2 * FT)] + [(DOWN, j) for j in range(8)])
NG = len(GROUPS)
G_OF = {g: i for i, g in enumerate(GROUPS)}
BANKS = 4
LN_EXP = "natural_log_exp_and_others"
DOWN_CUTS = ((0, 8), (8, 15), (15, FT))

UNITS = ([(XBC, j, 0) for j in range(8)] + [(UU, j, 0) for j in range(4)] + [(QQ, j, 0) for j in range(4)]
         + [(KK, j, 0) for j in range(4)] + [(VV, 0, v) for v in range(4)] + [(ZZ, j, 0) for j in range(4)]
         + [(GATE, j, 0) for j in range(24)] + [(BRANCH, j, 0) for j in range(0, 24, 2)]
         + [(OUT, j, 0) for j in range(8)] + [(UP, j, 0) for j in range(2 * FT)]
         + [(DOWN, j, c) for j in range(8) for c in range(3)])
NU = len(UNITS)
U_OF = {u: i for i, u in enumerate(UNITS)}
AHEAD = 3
NRAW, NMOD, NHL = 4, 2, 3
JOINT = 3
MODT = 6 * KT
MOD_HEAD = 2 * KT
MOD_G2 = 5 * KT
UP0 = U_OF[(UP, 0, 0)]
DOWN0 = U_OF[(DOWN, 0, 0)]
G2_EVERY = 5
G2_LAST = UP0 + G2_EVERY * (MODT - MOD_G2) - 1
HEAD_LAST = DOWN0 + MOD_HEAD + 1
PREP = HEAD_LAST + 1
POOL_LO = range(AHEAD, AHEAD + 8)
MIX0 = U_OF[(ZZ, 0, 0)]


def closing_unit(g):
    kind, j = GROUPS[g]
    return U_OF[{VV: (VV, 0, 3), BRANCH: (BRANCH, j - j % 2, 0), DOWN: (DOWN, j, 2)}.get(kind, (kind, j, 0))]


def lo_number(n):
    on_pool = n % NU in POOL_LO
    return on_pool, sum((i % NU in POOL_LO) == on_pool for i in range(n + 1))


def done_after(u):
    kind, j, part = UNITS[u]
    if kind == VV:
        return [G_OF[(VV, c)] for c in range(NCH)] if part == 3 else []
    if kind == BRANCH:
        return [G_OF[(BRANCH, j)], G_OF[(BRANCH, j + 1)]]
    if kind == DOWN:
        return [G_OF[(DOWN, j)]] if part == 2 else []
    return [G_OF[(kind, j)]]


def mod_after(l, u):
    if u < MOD_G2 - MOD_HEAD:
        return (l, MOD_HEAD + u)
    if UP0 <= u < DOWN0 and (u - UP0) % G2_EVERY == G2_EVERY - 1 and (u - UP0) // G2_EVERY < MODT - MOD_G2:
        return (l, MOD_G2 + (u - UP0) // G2_EVERY)
    m = u - DOWN0 - 2
    return (l + 1, m) if 0 <= m < MOD_HEAD and l + 1 < DEPTH else None


MODS = [(l, u) for l in range(DEPTH) for u in range(NU) if mod_after(l, u)]
MOD_NO = {lu: i for i, lu in enumerate(MODS)}
MOD_LEAD = 4


def stream_order():
    order = []
    for n in range(DEPTH * NU + MOD_LEAD):
        if n < DEPTH * NU:
            order.append((n // NU, "w", n % NU))
        l, u = divmod(n - MOD_LEAD, NU)
        if n >= MOD_LEAD and (l, u) in MOD_NO:
            order.append((l, "mod", u))
    return order


STREAM = stream_order()
NS = len(STREAM)
COLS = {}
for _u, (_k, _j, _c) in enumerate(UNITS):
    COLS[_u] = P * (DOWN_CUTS[_c][1] - DOWN_CUTS[_c][0]) if _k == DOWN else P * KT

PAR = {}
_at = 0
for _name, _n in (("n2g", KT), ("pscale", 4), ("subg", 1), ("li", 1), ("oml", 1),
                  ("cw", 24), ("cb", 8), ("ssdg", 4), ("ssdD", 4), ("bgate", 24), ("fw", 6 * FT), ("fb", 2 * FT),
                  ("dtb", 16), ("alog", 16), ("lam", 4 * QK), ("wdt", KT * 16), ("plw", 4 * P)):
    PAR[_name] = (_at, _n)
    _at += _n
NPAR = _at
NBIAS = DEPTH * (MODT + KT)

TAB = {}
_at = 0
for _name, _n in (("ident", P), ("ones", P), ("le", P), ("ge", P), ("gt", P), ("lt", P), ("negf", P), ("negb", P),
                  ("cos", LAT), ("sin", LAT), ("edge", 64), ("eps", 1)):
    TAB[_name] = (_at, _n)
    _at += _n
NTAB = _at

NATT = HEADS * NCH
NY = NCH * SSD_G
NMISC = 15
NCONV = 8 + 2 * FT
M_DT, M_DTT, M_SM, M_PW, M_ATT, M_SSD, M_N2 = 1, 2, 3, 4, 8, 12, 14
S_TASKS = ((0, 0), (1, 1), (2, 0), (2, 1))
ROTATE_SLOTS = (0, 1, 2, 3, 5, 6)
SLOT_PW, SLOT_X, SLOT_S, SLOT_Y = 4, 14, 17, 19
Y_SLOTS = 2
SLOT_RMS = SLOT_Y + Y_SLOTS * NY + 1
SLOT_SPLIT = U_OF[(GATE, 23, 0)] - MIX0


def scan_task(s, lag=0):
    y_, rest = divmod(s - lag - SLOT_Y, Y_SLOTS)
    return y_ if rest == 0 and 0 <= y_ < NY else None


def count(l, per, i):
    return l * per + i + 1


class Steps:

    def __init__(self, eng, sem):
        self.eng, self.sem, self.n = eng, sem, 0

    def then(self, ins):
        ins.then_inc(self.sem, 1)
        self.n += 1
        self.eng.wait_ge(self.sem, self.n)


def tables():
    t = np.zeros((P, NTAB), np.float32)

    def put(name, a):
        at, n = TAB[name]
        t[:, at:at + n] = a

    i, j = np.arange(P)[:, None], np.arange(P)[None, :]
    put("ident", i == j)
    put("ones", 1.0)
    put("le", i <= j)
    put("ge", i >= j)
    put("gt", i > j)
    put("lt", i < j)
    put("negf", np.where(j >= i, 0.0, NEG))
    put("negb", np.where(j <= i, 0.0, NEG))
    tok = np.arange(LAT)
    half = QK // 2
    inv = (np.float32(10000.0) ** (-np.arange(0, half, 2, dtype=np.float32) / np.float32(half))).astype(np.float32)
    ang = np.zeros((P, LAT), np.float32)
    sign = np.zeros((P, 1), np.float32)
    for p in range(P):
        d = p % QK
        pos = (tok // GRID_W if d < half else tok % GRID_W).astype(np.float32)
        ang[p] = pos * inv[d % (half // 2)]
        sign[p] = -1.0 if d % half < half // 2 else 1.0
    put("cos", np.cos(ang))
    put("sin", np.sin(ang) * sign)
    edge = np.zeros((4, 2, PADL), np.float32)
    for g, w in enumerate(WINDOWS):
        h = w // 2
        for k in range(PADL):
            edge[g, 0, k] = 1.0 / (min(k, h) + h)
            tail = PADL - k
            edge[g, 1, k] = 1.0 / (min(tail, h) + h)
    put("edge", edge.reshape(1, 64))
    put("eps", EPS)
    return t


def build(nc, wstream, whead, par, bias, tab, xs, xp, cvec, cvec_rows, kc, vc, st0, fng, y, newk, newv, news):
    ctx = ExitStack()
    with ctx:
        def sb(name, shape, dt=F32, where=ctx):
            return where.enter_context(nc.sbuf_tensor(name, shape, dt))

        def sem(name):
            return ctx.enter_context(nc.semaphore(name))

        raw = sb("raw", [P, NRAW, P * KT])
        rawm = sb("rawm", [P, NMOD, P * KT])
        wh = sb("wh", [P, NHL, P * KT], F32R)
        wl = sb("wl", [P, NHL, P * KT], F32R)
        x = sb("x", [P, KT, T])
        hh = sb("hh", [P, KT, T], F32R)
        hl = sb("hl", [P, KT, T], F32R)
        with ExitStack() as a:
            gates = sb("gates", [P, 24, T], where=a)
            xbc = sb("xbc", [P, 8, T], where=a)
            zz = sb("zz", [P, 4, T], where=a)
            ut = sb("ut", [P, 4, UW], where=a)
            ot = sb("ot", [P, HEADS, T], where=a)
        with ExitStack() as a:
            sb("under_gates", [P, 24, T], where=a)
            osh = sb("osh", [P, 4, T], F32R, where=a)
            osl = sb("osl", [P, 4, T], F32R, where=a)
        with ExitStack() as a:
            ah = sb("ah", [P, FT, T], F32R, where=a)
            al = sb("al", [P, FT, T], F32R, where=a)
        with ExitStack() as a:
            junk_front = sb("junk_front", [P, 2, D], where=a)
        with ExitStack() as a:
            head = sb("head", [P, MOD_HEAD, P * KT], where=a)
        sb("main_region", [P, 24 * T + 8 * T + 4 * T + 4 * UW + HEADS * T])
        with ExitStack() as a:
            qt = sb("qt", [P, HEADS, T], where=a)
            kt_ = sb("kt", [P, HEADS, PAST + T], where=a)
            vv = sb("vv", [P, 4, 4 * P], where=a)
            pr = sb("pr", [P, 2, 2, PAST + LAT], where=a)
            at_ = sb("at", [P, 2, PAST + LAT], where=a)
        with ExitStack() as a:
            xt = sb("xt", [P, NCH, 4 * P], where=a)
            bg = sb("bg", [P, NCH, 4 * P], where=a)
            hst = sb("hst", [P, 4, 4 * P], where=a)
            xw = sb("xw", [P, 4 * P], where=a)
            with ExitStack() as b:
                rst = sb("rst", [P, 4, T], where=b)
            ee = sb("ee", [P, 2, 4 * P], where=a)
            eb = sb("eb", [P, 2, 4 * P], where=a)
        with ExitStack() as a:
            junk_ffn = sb("junk_ffn", [P, 2, D], where=a)
            sb("under_crow", [P, 2 * HEADS * T + HEADS * PAST + 16 * P - 2 * D], where=a)
            crow = sb("crow", [P, 2, D], where=a)
        with ExitStack() as a:
            mh = sb("mh", [P, KT, T], F32R, where=a)
            ml = sb("ml", [P, KT, T], F32R, where=a)
        sb("mixer_region", [P, 2 * HEADS * T + HEADS * PAST + 16 * P + 6 * (PAST + LAT)])
        cv = sb("cv", [P, 2, T])
        th = sb("th", [P, 2, T])
        sqa = sb("sqa", [P, T])
        rs = sb("rs", [P, T])
        prm = sb("prm", [P, NPAR])
        tb = sb("tb", [P, NTAB])
        wdh = sb("wdh", [P, KT * 16], F32R)
        wdl = sb("wdl", [P, KT * 16], F32R)
        mod = sb("mod", [P, MODT, 2])
        macc = sb("macc", [P, MODT, 2])
        sc1 = sb("sc1", [P, KT, 2])
        sc2 = sb("sc2", [P, KT, 2])
        g1h = sb("g1h", [P, KT, 2])
        cs = sb("cs", [P, 2 * KT])
        csh = sb("csh", [P, 2 * KT])
        cst = sb("cst", [P, 2 * KT])
        bgh = sb("bgh", [P, 24])
        nlam = sb("nlam", [P, 1])
        lamt = sb("lamt", [P, 2, QK])
        lams = sb("lams", [P, 4])
        sg = sb("sg", [P, 1])
        eal = sb("eal", [P, 16])
        mxb = sb("mxb", [P, 2, 2])
        nmb = sb("nmb", [P, 2, 2])
        rsm = sb("rsm", [P, 2, 2])
        rcp = sb("rcp", [P, 3])
        dtv = sb("dtv", [P, 48])
        dte = sb("dte", [P, 48])
        dtt = sb("dtt", [P, 48])
        adt = sb("adt", [P, 48])
        sm = sb("sm", [P, 144])
        nac = sb("nac", [P, 48])
        ede = sb("ede", [P, 96])
        wdc = sb("wdc", [P, 48])
        fg = sb("fg", [P, KT])
        bm = sb("bm", [P, NBIAS])

        acc = [ctx.enter_context(nc.psum_tensor(f"acc{i}", [P, 512], F32)) for i in range(BANKS)]
        misc = ctx.enter_context(nc.psum_tensor("misc", [P, 512], F32))
        mix5 = ctx.enter_context(nc.psum_tensor("mix5", [P, 512], F32))
        mix6 = ctx.enter_context(nc.psum_tensor("mix6", [P, 512], F32))
        mix7 = ctx.enter_context(nc.psum_tensor("mix7", [P, 512], F32))
        dtc = gates[:, 13, :]
        end_state = [b[:, :, :].rearrange("p a t -> p (a t)")[:, 0:4 * P] for b in (th, cv)]
        modp = mix7[:, 0:2 * MODT]
        modq = mix6[:, 0:2 * MODT]
        mz = misc[:, 0:T]

        def prm_(name, i=0, n=1):
            at = PAR[name][0] + i
            return prm[:, at:at + n]

        def tab_(name):
            at, n = TAB[name]
            return tb[:, at:at + n]

        ident, ones, le, ge, gt, lt = (tab_(n) for n in ("ident", "ones", "le", "ge", "gt", "lt"))
        tri, neg = (le, ge), (tab_("negf"), tab_("negb"))
        cos, sin = tab_("cos"), tab_("sin")
        edge = tab_("edge").rearrange("p (g s k) -> p g s k", g=4, s=2)

        cs_in = sem("cs_in")
        x_in = sem("x_in")
        tab_in = sem("tab_in")
        head_in = [sem(f"head_in{j}") for j in range(KT)]
        head_done = sem("head_done")
        scale_ready = sem("scale_ready")
        fg_in = sem("fg_in")
        par_in = sem("par_in")
        cache_in = sem("cache_in")
        state_in = sem("state_in")
        raw_in = [sem(f"raw_in{i}") for i in range(NRAW)]
        mod_in = [sem(f"mod_in{i}") for i in range(NMOD)]
        hi_done = sem("hi_done")
        lo_done = sem("lo_done")
        pool_lo_done = sem("pool_lo_done")
        unit_used = sem("unit_used")
        mod_used = sem("mod_used")
        crow_in = sem("crow_in")
        crow_tanh = sem("crow_tanh")
        crow_ready = sem("crow_ready")
        cs_ready = sem("cs_ready")
        cs_tanh = sem("cs_tanh")
        cs_half = sem("cs_half")
        mod_read = sem("mod_read")
        misc_done = sem("misc_done")
        att_ss = sem("att_ss")
        z_ss = sem("z_ss")
        zeroed = sem("zeroed")
        sq_done = sem("sq_done")
        sq_sum = sem("sq_sum")
        rs_ready = sem("rs_ready")
        h_full = sem("h_full")
        h_hi = sem("h_hi")
        h_lo = sem("h_lo")
        x_new = sem("x_new")
        cv_init = sem("cv_init")
        cv_done = sem("cv_done")
        cv_tanh = sem("cv_tanh")
        cv_out = sem("cv_out")
        par_ready = sem("par_ready")
        lam_exp = sem("lam_exp")
        lam_sum = sem("lam_sum")
        wd_hi = sem("wd_hi")
        u_in = sem("u_in")
        pooled = sem("pooled")
        pads = sem("pads")
        op_done = sem("op_done")
        qk_in = sem("qk_in")
        qk_done = sem("qk_done")
        v_in = sem("v_in")
        z_tanh = sem("z_tanh")
        z_done = sem("z_done")
        dt_in = sem("dt_in")
        dt_raw = sem("dt_raw")
        dt_log = sem("dt_log")
        adt_done = sem("adt_done")
        sm_done = sem("sm_done")
        ede_done = sem("ede_done")
        wdc_done = sem("wdc_done")
        s_done = sem("s_done")
        nm_done = sem("nm_done")
        exp_done = sem("exp_done")
        a_done = sem("a_done")
        tr_done = sem("tr_done")
        at_done = sem("at_done")
        av_done = sem("av_done")
        o_done = sem("o_done")
        osq_done = sem("osq_done")
        ors_done = sem("ors_done")
        on_done = sem("on_done")
        xt_done = sem("xt_done")
        xt_in = sem("xt_in")
        xw_done = sem("xw_done")
        cst_done = sem("cst_done")
        st_done = sem("st_done")
        bc_done = sem("bc_done")
        d_done = sem("d_done")
        e_done = sem("e_done")
        m_done = sem("m_done")
        y_done = sem("y_done")
        yz_done = sem("yz_done")
        zsq_done = sem("zsq_done")
        zrs_done = sem("zrs_done")
        zn_done = sem("zn_done")
        g_done = sem("g_done")
        gb_done = sem("gb_done")
        mg_done = sem("mg_done")
        k_out = sem("k_out")
        v_out = sem("v_out")
        st_out = sem("st_out")
        y_ready = sem("y_ready")
        y_out = sem("y_out")
        dve_step = sem("dve_step")
        act_step = sem("act_step")
        pool_step = sem("pool_step")

        SP_N1, SP_OP, SP_OT, SP_Z, SP_MG, SP_N2, SP_FF = 0, 8, 12, 16, 20, 28, 36
        NSPLIT = SP_FF + FT
        F_N1, F_MG, F_N2, F_FF = 0, 8, 16, 24
        NFULL = F_FF + FT

        def raw_slot(u):
            return u % NRAW

        def raw_value(l, u):
            return 16 * (l * (NU // NRAW) + u // NRAW + 1)

        def wait_lo(eng, n):
            on_pool, number = lo_number(n)
            eng.wait_ge(pool_lo_done if on_pool else lo_done, number)

        def group_done(eng, l, g):
            eng.wait_ge(unit_used, count(l, NU, closing_unit(g)))

        def group_read(eng, l, g):
            kind, j = GROUPS[g]
            s_, per, i = {XBC: (cv_done, NCONV, j), UP: (cv_done, NCONV, 8 + j), UU: (u_in, 4, j), QQ: (qk_in, 8, j),
                          KK: (qk_in, 8, HEADS + j), VV: (v_in, NCH, j), ZZ: (z_done, 4, j), GATE: (g_done, 24, j),
                          BRANCH: (gb_done, 24, j), OUT: (x_new, 16, j), DOWN: (x_new, 16, KT + j)}[kind]
            eng.wait_ge(s_, count(l, per, i))

        def misc_read(eng, l, i):
            if i == 0 or i == M_N2:
                eng.wait_ge(rs_ready, count(l, 2, i == M_N2))
            elif i == M_DT:
                eng.wait_ge(dt_in, l + 1)
            elif i == M_DTT:
                eng.wait_ge(dt_raw, l + 1)
            elif i == M_SM:
                eng.wait_ge(sm_done, l + 1)
            elif i < M_ATT:
                eng.wait_ge(op_done, count(l, 4, i - M_PW))
            elif i < M_SSD:
                eng.wait_ge(att_ss, count(l, HEADS, i - M_ATT))
            else:
                eng.wait_ge(z_ss, count(l, 2, i - M_SSD))

        block = ctx.enter_context(nc.Block())

        @block.sync
        def _(sp):
            sp.dma_start(cs[:, :], cvec).then_inc(cs_in, 16)
            sp.dma_start(bm[:, :], bias).then_inc(cs_in, 16)
            sp.dma_start(x[:, :, 0:LAT], xs).then_inc(x_in, 16)
            sp.dma_start(x[:, :, CTX0:T], xp).then_inc(x_in, 16)
            sp.dma_start(tb[:, :], tab).then_inc(tab_in, 16)

            def load_head(j):
                sp.dma_start(head[:, 2 * j:2 * j + 2, :], whead[j].rearrange("p (a c) -> p a c", a=2)) \
                    .then_inc(head_in[j], 16)

            for j in range(KT // 2):
                load_head(j)
            for i, (l, kind, u) in enumerate(STREAM):
                if i == JOINT:
                    for j in range(KT // 2, KT):
                        load_head(j)
                if kind == "w":
                    if l or u >= NRAW:
                        wait_lo(sp, l * NU + u - NRAW)
                    sp.dma_start(raw[:, raw_slot(u), 0:COLS[u]], wstream[i, :, 0:COLS[u]]) \
                        .then_inc(raw_in[raw_slot(u)], 16)
                else:
                    n = MOD_NO[l, u]
                    if n >= NMOD:
                        sp.wait_ge(mod_used, n - NMOD + 1)
                    sp.dma_start(rawm[:, n % NMOD, :], wstream[i, :, :]).then_inc(mod_in[n % NMOD], 16)

        @block.gpsimd
        def _(pool):
            step = Steps(pool, pool_step)
            nc.gpsimd.memset(x[:, :, LAT:CTX0], 0.0).then_inc(zeroed, 1)
            nc.gpsimd.memset(cv[:, :, :], 0.0).then_inc(zeroed, 1)

            def sum_squares(l, first, base):
                for j in range(KT):
                    pool.wait_ge(sq_done, base + j + 1)
                    if j == 0:
                        if not first:
                            pool.wait_ge(misc_done, count(l, NMISC, 0))
                        nc.gpsimd.tensor_copy(sqa[:, :], th[:, 0, :]).then_inc(sq_sum, 1)
                    else:
                        pool.wait_ge(sq_sum, base + j)
                        nc.gpsimd.tensor_tensor(sqa[:, :], sqa[:, :], th[:, j % 2, :], ALU.add).then_inc(sq_sum, 1)

            def load_params(l):
                pool.dma_start(prm[:, :], par[l]).then_inc(par_in, 16)

            pool.dma_start(crow[:, :, :], cvec_rows).then_inc(crow_in, 16)
            load_params(0)
            pool.dma_start(fg[:, :], fng).then_inc(fg_in, 16)
            sum_squares(0, True, 0)
            for l in range(DEPTH):
                if l:
                    group_done(pool, l - 1, G_OF[(OUT, KT - 1)])
                pool.dma_start(kt_[:, :, 0:PAST], kc[l]).then_inc(cache_in, 16)
                pool.dma_start(vv[:, 0, :], vc[l]).then_inc(cache_in, 16)
                for u in POOL_LO:
                    pool.wait_ge(hi_done, count(l, NU, u))
                    s, n = (l * NU + u) % NHL, COLS[u]
                    nc.gpsimd.tensor_tensor(wl[:, s, 0:n], raw[:, raw_slot(u), 0:n], wh[:, s, 0:n].bitcast(F32),
                                            ALU.subtract).then_inc(pool_lo_done, 1)
                if l:
                    group_done(pool, l - 1, NG - 1)
                else:
                    pool.wait_ge(head_done, 2)
                for c0, c1 in ((0, PADL), (ULAT + LAT, UCTX), (UCTX + SEQ, UW)):
                    nc.gpsimd.memset(ut[:, :, c0:c1], 0.0)
                nc.gpsimd.memset(gates[:, 16:20, LAT:CTX0], 0.0)
                nc.gpsimd.memset(ot[:, :, LAT:CTX0], 0.0).then_inc(pads, 1)
                pool.wait_ge(pads, l + 1)
                tmp = [gates[:, 20:22, :].rearrange("p a t -> p (a t)")[:, 0:UW],
                       gates[:, 22:24, :].rearrange("p a t -> p (a t)")[:, 0:UW]]
                for j in range(4):
                    pool.wait_ge(u_in, count(l, 4, j))
                    step.then(nc.gpsimd.tensor_tensor(tmp[0][:, 1:UW], ut[:, j, 0:UW - 1], ut[:, j, 1:UW], ALU.add))
                    lo, cur = 1, 0
                    for i in range(j):
                        s = 1 << i
                        lo += s
                        hi = UW - (lo - 1)
                        step.then(nc.gpsimd.tensor_tensor(tmp[1 - cur][:, lo:hi], tmp[cur][:, lo - s:hi - s],
                                                          tmp[cur][:, lo + s:hi + s], ALU.add))
                        cur = 1 - cur
                    win = tmp[cur]
                    out = gates[:, 16 + j, :]
                    for (a, b), u0 in zip(SEGS, (ULAT, UCTX)):
                        n = b - a
                        step.then(nc.gpsimd.tensor_scalar(out[:, a:b], win[:, u0:u0 + n], 1.0 / WINDOWS[j], None, ALU.mult))
                        nc.gpsimd.tensor_tensor(out[:, a:a + PADL], win[:, u0:u0 + PADL], edge[:, j, 0, :], ALU.mult)
                        step.then(nc.gpsimd.tensor_tensor(out[:, b - PADL:b], win[:, u0 + n - PADL:u0 + n],
                                                          edge[:, j, 1, :], ALU.mult))
                        ins = nc.gpsimd.tensor_tensor(out[:, a:b], out[:, a:b], ut[:, j, u0:u0 + n], ALU.subtract)
                        if a == 0:
                            step.then(ins)
                        else:
                            ins.then_inc(pooled, 1)
                pool.wait_ge(qk_done, count(l, 2 * HEADS, 2 * HEADS - 1))
                pool.dma_start(newk[l], kt_[:, :, PAST + CTX0:PAST + T]).then_inc(k_out, 16)
                pool.wait_ge(v_in, count(l, NCH, NCH - 1))
                pool.dma_start(newv[l], vv[:, 3, :]).then_inc(v_out, 16)
                pool.wait_ge(av_done, count(l, NATT, NATT - 1))
                pool.wait_ge(k_out, 16 * (l + 1))
                pool.wait_ge(v_out, 16 * (l + 1))
                for d in range(2):
                    pool.dma_start(hst[:, d, :], st0[l, d]).then_inc(state_in, 16)
                for k in range(2):
                    pool.wait_ge(st_done, count(l, 4, 2 + k))
                    pool.dma_start(news[l, k], end_state[k]).then_inc(st_out, 16)
                for j in range(KT):
                    pool.wait_ge(gb_done, count(l, 24, KT + j))
                    nc.gpsimd.tensor_tensor(gates[:, j, :], gates[:, j, :], gates[:, KT + j, :], ALU.add).then_inc(mg_done, 1)
                sum_squares(l, False, KT * (2 * l + 1))
                group_done(pool, l, G_OF[(OUT, KT - 1)])
                pool.dma_start(crow[:, :, :], cvec_rows).then_inc(crow_in, 16)
                if l + 1 < DEPTH:
                    pool.wait_ge(h_full, count(l, NFULL, NFULL - 1))
                    load_params(l + 1)
                for j in range(KT):
                    pool.wait_ge(sq_done, KT * (2 * l + 2) + j + 1)
                    if j == 0:
                        pool.wait_ge(misc_done, count(l, NMISC, M_N2))
                        nc.gpsimd.tensor_copy(sqa[:, :], th[:, 0, :]).then_inc(sq_sum, 1)
                    else:
                        pool.wait_ge(sq_sum, KT * (2 * l + 2) + j)
                        nc.gpsimd.tensor_tensor(sqa[:, :], sqa[:, :], th[:, j % 2, :], ALU.add).then_inc(sq_sum, 1)
            for j in range(KT):
                pool.wait_ge(y_ready, j + 1)
                pool.dma_start(y[:, j, :], gates[:, j, :]).then_inc(y_out, 16)
            pool.wait_ge(y_out, 16 * KT)
            pool.wait_ge(st_out, 32 * DEPTH)
            pool.wait_ge(k_out, 16 * DEPTH)
            pool.wait_ge(v_out, 16 * DEPTH)

        @block.tensor
        def _(pe):
            mm = nc.tensor.matmul

            def mean_squares(l, i, nth):
                misc_turn(l, i)
                pe.wait_ge(sq_sum, KT * (nth + 1))
                mm(mz, ones, sqa[:, :], start=True, stop=True).then_inc(misc_done, 1)

            def modulation_head(half):
                bank = (modp, modq)[half]
                for j in range(half * KT // 2, (half + 1) * KT // 2):
                    if j == KT // 2 - 1:
                        mean_squares(0, 0, 0)
                    pe.wait_ge(head_in[j], 16)
                    for k in range(KT):
                        last = mm(bank[:, 2 * j:2 * j + 2], head[:, 2 * j, P * k:P * k + P],
                                  cs[:, 2 * k:2 * k + 2], start=(k == 0), stop=(k == KT - 1))
                last.then_inc(head_done, 1)

            def misc_turn(l, i):
                if i:
                    misc_read(pe, l, i - 1)
                elif l:
                    misc_read(pe, l - 1, NMISC - 1)

            def three(out, sh, sl, mhi, mlo, start, stop):
                mm(out, sh, mhi, start=start, stop=False)
                mm(out, sh, mlo, start=False, stop=False)
                return mm(out, sl, mhi, start=False, stop=stop)

            def unit(l, u):
                kind, j, part = UNITS[u]
                s = (l * NU + u) % NHL
                wait_lo(pe, l * NU + u)

                def blk(b):
                    return wh[:, s, P * b:P * b + P], wl[:, s, P * b:P * b + P]

                def open_bank(g):
                    if g >= BANKS:
                        group_read(pe, l, g - BANKS)
                    return acc[g % BANKS]

                if kind == VV:
                    for kk in range(2):
                        k = 2 * part + kk
                        for c in range(NCH):
                            g = G_OF[(VV, c)]
                            bank = open_bank(g) if k == 0 else acc[g % BANKS]
                            tok = slice(CHUNK0[c], CHUNK0[c] + P)
                            wsl = slice(4 * P * kk, 4 * P * kk + 4 * P)
                            last = three(bank[:, :], hh[:, k, tok], hl[:, k, tok], wh[:, s, wsl], wl[:, s, wsl],
                                         k == 0, k == KT - 1)
                elif kind == BRANCH:
                    b = j // KT
                    src = ((hh, hl, 0), (hh, hl, 4), (osh, osl, 0))[b]
                    for jj in range(2):
                        g = G_OF[(BRANCH, j + jj)]
                        bank = open_bank(g)
                        for k in range(4):
                            if jj == 0 and j % KT == 0:
                                pe.wait_ge(h_lo, count(l, NSPLIT, (SP_OP, SP_OT, SP_Z)[b] + k))
                            w1, w2 = blk(4 * jj + k)
                            last = three(bank[:, 0:T], w1, w2, src[0][:, src[2] + k, :], src[1][:, src[2] + k, :],
                                         k == 0, k == 3)
                elif kind == DOWN:
                    g = G_OF[(DOWN, j)]
                    k0, k1 = DOWN_CUTS[part]
                    bank = open_bank(g) if part == 0 else acc[g % BANKS]
                    for k in range(k0, k1):
                        if j == 0:
                            pe.wait_ge(h_lo, count(l, NSPLIT, SP_FF + k))
                        w1, w2 = blk(k - k0)
                        last = three(bank[:, 0:T], w1, w2, ah[:, k, :], al[:, k, :], k == 0, k == FT - 1)
                else:
                    g = G_OF[(kind, j)]
                    bank = open_bank(g)
                    first = SP_MG if (kind, j) == (OUT, 0) else None
                    srch, srcl = (mh, ml) if kind == OUT else (hh, hl)
                    for k in range(KT):
                        if first is not None:
                            pe.wait_ge(h_lo, count(l, NSPLIT, first + k))
                        w1, w2 = blk(k)
                        last = three(bank[:, 0:T], w1, w2, srch[:, k, :], srcl[:, k, :], k == 0, k == KT - 1)
                last.then_inc(unit_used, 1)

            def joint(l, u0, split0):
                kind = UNITS[u0][0]
                banks = []
                for i in range(JOINT):
                    wait_lo(pe, l * NU + u0 + i)
                    g = G_OF[(kind, i)]
                    if g >= BANKS:
                        group_read(pe, l, g - BANKS)
                    banks.append(acc[g % BANKS])

                def product(i, k):
                    s = (l * NU + u0 + i) % NHL
                    return three(banks[i][:, 0:T], wh[:, s, P * k:P * k + P], wl[:, s, P * k:P * k + P], hh[:, k, :],
                                 hl[:, k, :], k == 0, k == KT - 1)

                for k in range(KT - 2):
                    if l == 0 and u0 == 0 and k == KT // 2:
                        modulation_head(1)
                    pe.wait_ge(h_lo, count(l, NSPLIT, split0 + k))
                    for i in range(JOINT):
                        product(i, k)
                pe.wait_ge(h_lo, count(l, NSPLIT, split0 + KT - 1))
                for i in range(JOINT):
                    product(i, KT - 2)
                    product(i, KT - 1).then_inc(unit_used, 1)

            def time_steps(l):
                misc_turn(l, M_DT)
                pe.wait_ge(par_ready, l + 1)
                for k in range(KT):
                    ws = slice(16 * k, 16 * k + 16)
                    last = three(mz[0:16, :], wdh[:, ws], wdl[:, ws], hh[:, k, :], hl[:, k, :], k == 0, k == KT - 1)
                last.then_inc(misc_done, 1)

            def time_transposes(l):
                misc_turn(l, M_DTT)
                for c in range(NCH):
                    last = nc.tensor.transpose(mz[:, 16 * c:16 * c + 16], dtc[0:16, CHUNK0[c]:CHUNK0[c] + P],
                                               ident[0:16, 0:16])
                last.then_inc(misc_done, 1)

            def cumulative(l):
                misc_turn(l, M_SM)
                pe.wait_ge(adt_done, l + 1)
                a3 = adt[:, :].rearrange("p (c h) -> p c h", c=NCH)
                n = NCH * SSD_H
                for i, (m_, d) in enumerate(((le, 0), (ge, 1), (gt, 0), (lt, 1))):
                    mm(mz[:, n * i:n * i + n], m_, a3[:, :, SSD_H * d:SSD_H * d + SSD_H], start=True, stop=True)
                mm(mz[:, 4 * n:6 * n], ones, adt[:, :], start=True, stop=True).then_inc(misc_done, 1)

            def scores(l, i):
                h, t = divmod(i, NCH)
                nk, k0 = (PAST + LAT, 0) if t < 2 else (SEQ, PAST + CTX0)
                if t == 0:
                    pe.wait_ge(qk_done, count(l, 2 * HEADS, 2 * h + 1))
                if i == 0:
                    pe.wait_ge(cache_in, 32 * (l + 1))
                if i:
                    pe.wait_ge(exp_done, count(l, NATT, i - 1))
                for m_, bank in enumerate((mix5, mix6)):
                    q = slice(QK * m_, QK * m_ + QK)
                    last = mm(bank[:, 0:nk], qt[q, h, CHUNK0[t]:CHUNK0[t] + P], kt_[q, h, k0:k0 + nk],
                              start=True, stop=True)
                last.then_inc(s_done, 1)

            def transposes(l, i):
                n = 3 if i % NCH < 2 else 1
                pe.wait_ge(a_done, count(l, NATT, i))
                if i:
                    pe.wait_ge(at_done, count(l, NATT, i - 1))
                elif l == 0:
                    pe.wait_ge(mod_read, 2)
                for b in range(n):
                    last = nc.tensor.transpose(mix7[:, P * b:P * b + P], pr[:, i % 2, 0, P * b:P * b + P], ident)
                last.then_inc(tr_done, 1)

            def values(l, i):
                h, t = divmod(i, NCH)
                if i == 0:
                    pe.wait_ge(v_in, count(l, NCH, NCH - 1))
                pe.wait_ge(at_done, count(l, NATT, i))
                pe.wait_ge(exp_done, count(l, NATT, min(i + 1, NATT - 1)))
                if i:
                    pe.wait_ge(o_done, count(l, NATT, i - 1))
                tiles = (0, 1, 2) if t < 2 else (3,)
                for b, v in enumerate(tiles):
                    last = mm(mix5[:, 3 * P:4 * P], vv[:, v, P * h:P * h + P], at_[:, i % 2, P * b:P * b + P],
                              start=(b == 0), stop=(b == len(tiles) - 1))
                last.then_inc(av_done, 1)

            def chunk(l, c):
                tok = slice(CHUNK0[c], CHUNK0[c] + P)
                pe.wait_ge(cv_out, count(l, 8 + FT, 7))
                if c:
                    pe.wait_ge(xt_in, count(l, NCH, c - 1))
                else:
                    pe.wait_ge(o_done, count(l, NATT, NATT - 1))
                for j in range(4):
                    nc.tensor.transpose(mix5[:, P * j:P * j + P], xbc[:, j, tok], ident)
                for g in range(2):
                    nc.tensor.transpose(mix6[:, P * g:P * g + P], xbc[:, 4 + g, tok], ident)
                for g in range(2):
                    last = mm(mix6[:, P * (2 + g):P * (3 + g)], xbc[:, 4 + g, tok], xbc[:, 6 + g, tok],
                              start=True, stop=True)
                last.then_inc(xt_done, 1)

            def chunk_state(l, k):
                c, d = S_TASKS[k]
                pe.wait_ge(xw_done, count(l, 4, k))
                if k:
                    pe.wait_ge(st_done, count(l, 4, k - 1))
                else:
                    pe.wait_ge(at_done, count(l, NATT, NATT - 1))
                for g in range(2):
                    last = mm(mix7[:, 2 * P * g:2 * P * g + 2 * P], bg[:, c, P * g:P * g + P],
                              xw[:, 2 * P * g:2 * P * g + 2 * P], start=True, stop=True)
                last.then_inc(cst_done, 1)

            def rows(l, y_):
                c, g = divmod(y_, 2)
                if y_:
                    pe.wait_ge(d_done, count(l, NY, y_ - 1))
                    pe.wait_ge(e_done, count(l, NY, y_ - 1))
                else:
                    pe.wait_ge(xt_in, count(l, NCH, NCH - 1))
                for d, bank in enumerate((mix5, mix6)):
                    for i in range(4):
                        col = 16 * c + SSD_H * d + 4 * g + i
                        last = mm(bank[:, P * i:P * i + P], adt[:, col:col + 1].to_broadcast([P, P]), tri[d],
                                  start=True, stop=True)
                last.then_inc(bc_done, 1)

            def scan_out(l, y_):
                c, g = divmod(y_, 2)
                pe.wait_ge(m_done, count(l, NY, y_))
                if y_:
                    pe.wait_ge(yz_done, count(l, NY, y_ - 1))
                else:
                    pe.wait_ge(st_done, count(l, 4, 3))
                    pe.wait_ge(state_in, 32 * (l + 1))
                for i in range(4):
                    h = 4 * g + i
                    out = mix7[64 * (i % 2):64 * (i % 2) + 64, P * (i // 2):P * (i // 2) + P]
                    hs = slice(SSD_P * h, SSD_P * h + SSD_P)
                    ms = slice(P * i, P * i + P)
                    terms = [(xt[:, c, hs], ee[:, d, ms]) for d in range(2)]
                    if c < 2:
                        terms += [(hst[:, (0, 3)[d] if c == 0 else (2, 1)[d], hs], eb[:, d, ms]) for d in range(2)]
                    for n, (s_, m_) in enumerate(terms):
                        last = mm(out, s_, m_, start=(n == 0), stop=(n == len(terms) - 1))
                last.then_inc(y_done, 1)

            def mixers(l, s):
                if 2 <= s < NATT + 2:
                    values(l, s - 2)
                if 1 <= s < NATT + 1:
                    transposes(l, s - 1)
                if s < NATT:
                    scores(l, s)
                if s == 0:
                    time_steps(l)
                if s == 1:
                    time_transposes(l)
                if s == 3:
                    cumulative(l)
                if SLOT_PW <= s < SLOT_PW + 4:
                    j = s - SLOT_PW
                    misc_turn(l, M_PW + j)
                    pe.wait_ge(pooled, count(l, 4, j))
                    mm(mz, prm_("plw", P * j, P), gates[:, 16 + j, :], start=True, stop=True).then_inc(misc_done, 1)
                if SLOT_X <= s < SLOT_X + NCH:
                    if s == SLOT_X:
                        pe.wait_ge(exp_done, count(l, NATT, NATT - 1))
                    chunk(l, s - SLOT_X)
                if SLOT_X <= s < SLOT_X + HEADS:
                    h = s - SLOT_X
                    misc_turn(l, M_ATT + h)
                    pe.wait_ge(osq_done, l + 1)
                    mm(mz, ones, rst[:, h, :], start=True, stop=True).then_inc(misc_done, 1)
                if SLOT_S <= s < SLOT_S + 4:
                    chunk_state(l, s - SLOT_S)
                if scan_task(s, Y_SLOTS) is not None:
                    scan_out(l, scan_task(s, Y_SLOTS))
                if scan_task(s) is not None:
                    rows(l, scan_task(s))
                if SLOT_RMS <= s < SLOT_RMS + 2:
                    g = s - SLOT_RMS
                    misc_turn(l, M_SSD + g)
                    pe.wait_ge(zsq_done, l + 1)
                    mm(mz, ones, rst[:, 2 * g, :], start=True, stop=False)
                    mm(mz, ones, rst[:, 2 * g + 1, :], start=False, stop=True).then_inc(misc_done, 1)

            pe.wait_ge(cs_ready, 1)
            pe.wait_ge(tab_in, 16)
            modulation_head(0)
            for l in range(DEPTH):
                if l:
                    mean_squares(l, 0, 2 * l)
                for u in range(NU):
                    if u in (0, UP0):
                        if u:
                            mean_squares(l, M_N2, 2 * l + 1)
                        joint(l, u, SP_N2 if u else SP_N1)
                    elif u not in (1, 2, UP0 + 1, UP0 + 2):
                        unit(l, u)
                    if MIX0 <= u <= MIX0 + SLOT_RMS + 1:
                        mixers(l, u - MIX0)
            misc_turn(DEPTH, 0)
            pe.wait_ge(sq_sum, KT * (2 * DEPTH + 1))
            mm(mz, ones, sqa[:, :], start=True, stop=True).then_inc(misc_done, 1)

        @block.scalar
        def _(act):
            af = nc.scalar.activation
            step = Steps(act, act_step)
            eps = tab_("eps")

            def hi(l, u):
                act.wait_ge(raw_in[raw_slot(u)], raw_value(l, u))
                if l * NU + u >= NHL:
                    act.wait_ge(unit_used, l * NU + u - NHL + 1)
                s, n = (l * NU + u) % NHL, COLS[u]
                af(wh[:, s, 0:n], raw[:, raw_slot(u), 0:n], ACT.Copy).then_inc(hi_done, 1)

            def inv_rms(l, i, n):
                act.wait_ge(misc_done, count(l, NMISC, i))
                if i:
                    act.wait_ge(h_full, count(l, NFULL, F_N1 + KT - 1))
                elif l:
                    act.wait_ge(h_full, count(l - 1, NFULL, F_N2 + KT - 1))
                step.then(af(rs[:, :], mz, ACT.Ln, bias=eps, scale=1.0 / n))
                af(rs[:, :], rs[:, :], ACT.Exp, scale=-0.5).then_inc(rs_ready, 1)

            def high(l, full, dst, src):
                if full is not None:
                    act.wait_ge(h_full, count(l, NFULL, full))
                af(dst, src, ACT.Copy).then_inc(h_hi, 1)

            def ahead(l, u):
                n = l * NU + u + AHEAD
                if n < DEPTH * NU:
                    hi(n // NU, n % NU)

            def norm(l, nth, split0, scale, shift0):
                for j in range(KT):
                    b = cv[:, j % 2, :]
                    act.wait_ge(h_full, count(l, NFULL, (F_N2 if nth else F_N1) + j))
                    act.wait_ge(scale_ready, 2 * l + 3 if nth else 2 * l + 2 if l or j >= KT // 2 else 1)
                    for v, (a0, a1) in enumerate(SEGS):
                        last = af(b[:, a0:a1], b[:, a0:a1], ACT.Identity, bias=mod[:, shift0 + j, v:v + 1],
                                  scale=scale[:, j, v:v + 1])
                    step.then(last)
                    high(l, None, hh[:, j, :], b)

            def params(l):
                act.wait_ge(par_in, 16 * (l + 1))
                if l:
                    act.wait_ge(wdc_done, l)
                af(eal[:, :], prm_("alog", 0, 16), ACT.Exp)
                af(wdh[:, :], prm_("wdt", 0, KT * 16), ACT.Copy).then_inc(wd_hi, 1)
                act.wait_ge(lam_sum, l + 1)
                af(lams[:, 2:4], lams[:, 0:2], ACT.Exp).then_inc(lam_exp, 1)

            def row_tanh(n):
                act.wait_ge(crow_in, 16 * (n + 1))
                for v in range(2):
                    if v:
                        act.wait_ge(crow_ready, 2 * n + v)
                    af(junk_ffn[:, 0, :], crow[:, v, :], ACT.Tanh, scale=0.5).then_inc(crow_tanh, 1)

            def square(first, j, after):
                if after is not None:
                    act.wait_ge(x_new, after + 1)
                if j >= 2:
                    act.wait_ge(sq_sum, first + j - 1)
                af(th[:, j % 2, :], x[:, j, :], ACT.Square).then_inc(sq_done, 1)

            def evac(l, g):
                kind, j = GROUPS[g]
                bank = acc[g % BANKS]
                group_done(act, l, g)
                if kind in (XBC, UP):
                    n = j if kind == XBC else 8 + j
                    w, b = ("cw", "cb") if kind == XBC else ("fw", "fb")
                    b_ = j % 2
                    tile = j if kind == XBC else (j // 2 + FT * (j % 2))
                    if kind == XBC and j < 2 or kind == UP and j < 2:
                        act.wait_ge(h_lo, count(l, NSPLIT, (SP_N1 if kind == XBC else SP_N2) + KT - 1))
                    elif kind == UP and b_ == 1:
                        act.wait_ge(h_lo, count(l, NSPLIT, SP_FF + j // 2 - 1))
                    else:
                        act.wait_ge(cv_out, count(l, 8 + FT, j - 2 if kind == XBC else 8 + j // 2 - 1))
                    af(cv[:, b_, :], bank[:, 0:T], ACT.Identity, bias=prm_(b, tile), scale=prm_(w, 3 * tile + 1)) \
                        .then_inc(cv_init, 1)
                elif kind == UU:
                    act.wait_ge(pads, l + 1)
                    af(ut[:, j, ULAT:ULAT + LAT], bank[:, 0:LAT], ACT.Copy)
                    af(ut[:, j, UCTX:UCTX + SEQ], bank[:, CTX0:T], ACT.Copy).then_inc(u_in, 1)
                elif kind in (QQ, KK):
                    dst = qt[:, j, :] if kind == QQ else kt_[:, j, PAST:PAST + T]
                    af(dst, bank[:, 0:T], ACT.Copy).then_inc(qk_in, 1)
                elif kind == VV:
                    af(vv[:, 1 + j, :], bank[:, :], ACT.Copy).then_inc(v_in, 1)
                elif kind == ZZ:
                    if j < 2:
                        act.wait_ge(cv_out, count(l, 8 + FT, 7))
                    else:
                        act.wait_ge(z_done, count(l, 4, j - 2))
                    af(th[:, j % 2, :], bank[:, 0:T], ACT.Tanh, scale=0.5).then_inc(z_tanh, 1)
                elif kind == GATE:
                    if j >= 16:
                        act.wait_ge(op_done, count(l, 4, 3))
                    af(gates[:, j, :], bank[:, 0:T], ACT.Tanh, bias=bgh[:, j:j + 1], scale=0.5).then_inc(g_done, 1)

            def conv_silu(l, g):
                kind, j = GROUPS[g]
                n = j if kind == XBC else 8 + j
                if kind == XBC or kind == UP and j % 2 == 0:
                    act.wait_ge(cv_done, count(l, NCONV, n))
                    b_ = j % 2
                    if kind == UP and j:
                        act.wait_ge(h_full, count(l, NFULL, F_FF + j // 2 - 1))
                    af(th[:, b_, :], cv[:, b_, :], ACT.Tanh).then_inc(cv_tanh, 1)

            def probabilities(l, i):
                nk = PAST + LAT if i % NCH < 2 else SEQ
                act.wait_ge(nm_done, count(l, NATT, i))
                if i >= 2:
                    act.wait_ge(tr_done, count(l, NATT, i - 2))
                    act.wait_ge(a_done, count(l, NATT, i - 2))
                for m_, bank in enumerate((mix5, mix6)):
                    last = af(pr[:, i % 2, m_, 0:nk], bank[:, 0:nk], ACT.Exp, bias=nmb[:, i % 2, m_:m_ + 1],
                              scale=SCALE, accum_out=rsm[:, i % 2, m_:m_ + 1])
                last.then_inc(exp_done, 1)

            def mixers(l, s):
                if 2 <= s < NATT + 2:
                    i = s - 2
                    h, t = divmod(i, NCH)
                    act.wait_ge(av_done, count(l, NATT, i))
                    if s < NATT:
                        act.wait_ge(nm_done, count(l, NATT, s))
                    af(ot[:, h, CHUNK0[t]:CHUNK0[t] + P], mix5[:, 3 * P:4 * P], ACT.Copy).then_inc(o_done, 1)
                if 1 <= s < NATT + 1:
                    i = s - 1
                    n = P * (3 if i % NCH < 2 else 1)
                    act.wait_ge(tr_done, count(l, NATT, i))
                    if i >= 2:
                        act.wait_ge(av_done, count(l, NATT, i - 2))
                    af(at_[:, i % 2, 0:n], mix7[:, 0:n], ACT.Copy).then_inc(at_done, 1)
                if s < NATT:
                    probabilities(l, s)
                if s == 0:
                    act.wait_ge(misc_done, count(l, NMISC, M_DT))
                    af(dtc[0:16, :], mz[0:16, :], ACT.Copy).then_inc(dt_in, 1)
                if s == 2:
                    act.wait_ge(dt_raw, l + 1)
                    step.then(af(dte[:, :], dte[:, :], ACT.Exp))
                    af(dte[:, :], dte[:, :], ACT.Ln, bias=1.0).then_inc(dt_log, 1)
                if s == 3:
                    act.wait_ge(sm_done, l + 1)
                    af(ede[:, :], sm[:, 48:144], ACT.Exp).then_inc(ede_done, 1)
                if s == SLOT_X:
                    act.wait_ge(o_done, count(l, NATT, NATT - 1))
                    act.wait_ge(a_done, count(l, NATT, NATT - 1))
                    act.wait_ge(av_done, count(l, NATT, NATT - 1))
                    act.wait_ge(k_out, 16 * (l + 1))
                    act.wait_ge(v_out, 16 * (l + 1))
                    af(rst[:, :, :], ot[:, :, :], ACT.Square).then_inc(osq_done, 1)
                if SLOT_X <= s < SLOT_X + NCH:
                    c = s - SLOT_X
                    act.wait_ge(xt_done, count(l, NCH, c))
                    af(xt[:, c, :], mix5[:, :], ACT.Copy)
                    af(bg[:, c, :], mix6[:, :], ACT.Copy).then_inc(xt_in, 1)
                if SLOT_X <= s < SLOT_X + HEADS:
                    h = s - SLOT_X
                    act.wait_ge(misc_done, count(l, NMISC, M_ATT + h))
                    af(rst[:, h, :], mz, ACT.Copy).then_inc(att_ss, 1)
                    if h == HEADS - 1:
                        act.wait_ge(att_ss, count(l, HEADS, h))
                        act.preload_act_table_set(LN_EXP)
                        step.then(af(rst[:, :, :], rst[:, :, :], ACT.Ln, bias=eps, scale=1.0 / P))
                        af(rst[:, :, :], rst[:, :, :], ACT.Exp, scale=-0.5).then_inc(ors_done, 1)
                if SLOT_S + 2 <= s < SLOT_S + 4:
                    k = s - SLOT_S
                    act.wait_ge(cst_done, count(l, 4, k))
                    act.wait_ge(on_done, l + 1)
                    act.wait_ge(z_done, count(l, 4, 3))
                    af(end_state[k - 2], mix7[:, :], ACT.Copy).then_inc(st_done, 1)
                if scan_task(s) is not None:
                    y_ = scan_task(s)
                    act.wait_ge(bc_done, count(l, NY, y_))
                    act.wait_ge(d_done, count(l, NY, y_))
                    if y_ // 2 < 2:
                        if y_:
                            act.wait_ge(y_done, count(l, NY, y_ - 1))
                        for d, bank in enumerate((mix5, mix6)):
                            af(eb[:, d, :], bank[:, :], ACT.Exp)
                    af(ee[:, :, :], ee[:, :, :], ACT.Exp).then_inc(e_done, 1)
                if s == SLOT_RMS - 1:
                    act.wait_ge(yz_done, count(l, NY, NY - 1))
                    act.wait_ge(y_done, count(l, NY, NY - 1))
                    af(rst[:, :, :], zz[:, :, :], ACT.Square).then_inc(zsq_done, 1)
                if SLOT_RMS <= s < SLOT_RMS + 2:
                    g = s - SLOT_RMS
                    act.wait_ge(misc_done, count(l, NMISC, M_SSD + g))
                    af(rst[:, 2 * g, :], mz, ACT.Copy).then_inc(z_ss, 1)
                    if g == 1:
                        act.preload_act_table_set(LN_EXP)
                        act.wait_ge(z_ss, count(l, 2, g))
                        for g_ in range(2):
                            step.then(af(rst[:, 2 * g_, :], rst[:, 2 * g_, :], ACT.Ln, bias=eps, scale=0.5 / P))
                            last = af(rst[:, 2 * g_, :], rst[:, 2 * g_, :], ACT.Exp, scale=-0.5)
                        last.then_inc(zrs_done, 1)

            act.wait_ge(cs_half, 1)
            af(cst[:, :], csh[:, :], ACT.Tanh).then_inc(cs_tanh, 1)
            row_tanh(0)
            act.wait_ge(x_in, 32)
            act.wait_ge(zeroed, 2)
            for j in range(KT):
                square(0, j, None)
            act.wait_ge(tab_in, 16)
            for l in range(DEPTH):
                inv_rms(l, 0, D)
                if l == 0:
                    for u in range(AHEAD):
                        hi(l, u)
                norm(l, 0, SP_N1, sc1, 0)
                if l == 0:
                    params(l)
                act.wait_ge(par_ready, l + 1)
                for u in range(NU):
                    if u == UP0:
                        inv_rms(l, M_N2, D)
                        norm(l, 1, SP_N2, sc2, 3 * KT)
                        row_tanh(l + 1)
                    if u == PREP and l + 1 < DEPTH:
                        params(l + 1)
                    if UNITS[u] in ((OUT, 0, 0), (DOWN, 4, 2)):
                        act.preload_act_table_set(LN_EXP)
                    if u in (0, UP0):
                        ahead(l, u)
                    done = done_after(u)
                    for g in done:
                        if GROUPS[g][0] in (XBC, UU, QQ, KK, VV, ZZ, GATE, UP):
                            evac(l, g)
                    if u not in (0, UP0):
                        ahead(l, u)
                    for g in done:
                        kind, j = GROUPS[g]
                        if kind in (XBC, UP):
                            conv_silu(l, g)
                            if kind == UP and j % 2:
                                high(l, F_FF + j // 2, ah[:, j // 2, :], cv[:, 1, :])
                        if kind in (OUT, DOWN):
                            first = KT * (2 * l + (kind == DOWN))
                            square(KT + first, j, first + j)
                        if kind == BRANCH and j >= 2 * KT:
                            high(l, F_MG + j - 2 * KT, mh[:, j - 2 * KT, :], cv[:, j % 2, :])
                    if MIX0 <= u <= MIX0 + SLOT_RMS + 1:
                        s = u - MIX0
                        if s == SLOT_SPLIT:
                            group_done(act, l, G_OF[(GATE, 23)])
                            act.wait_ge(op_done, count(l, 4, 3))
                            for i in range(4):
                                high(l, None, hh[:, i, :], ut[:, i, 0:T])
                        mixers(l, s)
                        if s == SLOT_SPLIT + 1:
                            act.wait_ge(on_done, l + 1)
                            for i in range(4):
                                high(l, None, hh[:, 4 + i, :], ot[:, i, :])
                        if s == SLOT_RMS + 1:
                            for i in range(4):
                                act.wait_ge(zn_done, count(l, 4, i))
                                high(l, None, osh[:, i, :], zz[:, i, :])
            inv_rms(DEPTH, 0, D)

        @block.vector
        def _(dve):
            ts, tt, stt = nc.vector.tensor_scalar, nc.vector.tensor_tensor, nc.vector.scalar_tensor_tensor
            step = Steps(dve, dve_step)

            def lo(l, u):
                if u in POOL_LO:
                    return
                dve.wait_ge(hi_done, count(l, NU, u))
                s, n = (l * NU + u) % NHL, COLS[u]
                tt(wl[:, s, 0:n], raw[:, raw_slot(u), 0:n], wh[:, s, 0:n].bitcast(F32), ALU.subtract).then_inc(lo_done, 1)

            def low(l, i, dst, src, high_):
                dve.wait_ge(h_hi, count(l, NSPLIT, i))
                tt(dst, src, high_.bitcast(F32), ALU.subtract).then_inc(h_lo, 1)

            def ahead(l, u):
                n = l * NU + u + AHEAD
                if n < DEPTH * NU:
                    lo(n // NU, n % NU)

            def norm(l, nth, split0, after_half=None):
                dve.wait_ge(rs_ready, 2 * l + nth + 1)
                for j in range(KT):
                    if j >= 2:
                        dve.wait_ge(h_lo, count(l, NSPLIT, split0 + j - 2))
                    tt(cv[:, j % 2, :], x[:, j, :], rs[:, :], ALU.mult).then_inc(h_full, 1)
                    if j:
                        low(l, split0 + j - 1, hl[:, j - 1, :], cv[:, (j - 1) % 2, :], hh[:, j - 1, :])
                    if j == KT // 2 and after_half:
                        after_half()
                low(l, split0 + KT - 1, hl[:, KT - 1, :], cv[:, (KT - 1) % 2, :], hh[:, KT - 1, :])

            def biased(bank, lb, t0, t1):
                at = MODT * lb
                return tt(mod[:, t0:t1, :], bank[:, 2 * t0:2 * t1].rearrange("p (t v) -> p t v", v=2),
                          bm[:, at + t0:at + t1].unsqueeze(2).to_broadcast([P, t1 - t0, 2]), ALU.add)

            def rows_silu(n):
                for v in range(2):
                    dve.wait_ge(crow_tanh, 2 * n + v + 1)
                    stt(out=crow[:, v, :], in0=junk_ffn[:, 0, :], scalar=1.0, in1=crow[:, v, :], op0=ALU.add,
                        op1=ALU.mult).then_inc(crow_ready, 1)
                dve.wait_ge(crow_ready, 2 * n + 2)

            def modulation(l, u):
                if (l, u) not in MOD_NO:
                    return
                n = MOD_NO[l, u]
                m = mod_after(l, u)[1]
                junk = junk_front if u < UP0 else junk_ffn
                dve.wait_ge(mod_in[n % NMOD], 16 * (n // NMOD + 1))
                for v in range(2):
                    last = stt(out=junk[:, v, :], in0=rawm[:, n % NMOD, :], scalar=1.0, in1=crow[:, v, :], op0=ALU.mult,
                               op1=ALU.mult, accum_out=macc[:, m, v:v + 1])
                last.then_inc(mod_used, 1)
                dve.wait_ge(mod_used, n + 1)

            def summed(lb, t0, t1):
                at = MODT * lb
                step.then(stt(out=mod[:, t0:t1, :], in0=macc[:, t0:t1, :], scalar=0.5,
                              in1=bm[:, at + t0:at + t1].unsqueeze(2).to_broadcast([P, t1 - t0, 2]), op0=ALU.mult,
                              op1=ALU.add))

            def scale_of(dst, weight, t0, j0=0, j1=KT):
                step.then(ts(dst[:, j0:j1, :], mod[:, t0 + j0:t0 + j1, :], 1.0, None, ALU.add))
                return tt(dst[:, j0:j1, :], dst[:, j0:j1, :],
                          weight[:, j0:j1].unsqueeze(2).to_broadcast([P, j1 - j0, 2]), ALU.mult)

            def norm1_weight(l):
                at = DEPTH * MODT + l * KT
                return bm[:, at:at + KT]

            def head_half(half):
                j0, j1 = half * KT // 2, (half + 1) * KT // 2
                for j in range(j0, j1):
                    dve.wait_ge(head_in[j], 16)
                    for v, junk in enumerate((junk_ffn[:, 0, :], vv[:, 1:3, :].rearrange("p a c -> p (a c)"))):
                        step.then(stt(out=junk, in0=head[:, 2 * j + 1, :], scalar=1.0, in1=crow[:, v, :], op0=ALU.mult,
                                      op1=ALU.mult, accum_out=macc[:, KT + j, v:v + 1]))
                summed(0, KT + j0, KT + j1)
                dve.wait_ge(head_done, half + 1)
                biased((modp, modq)[half], 0, j0, j1).then_inc(mod_read, 1)
                dve.wait_ge(mod_read, half + 1)
                scale_of(sc1, norm1_weight(0), KT, j0, j1).then_inc(scale_ready, 1)

            def params(l):
                dve.wait_ge(par_in, 16 * (l + 1))
                lp = prm_("lam", 0, 4 * QK).rearrange("p (a b d) -> p a b d", a=2, b=2)
                step.then(tt(lamt[:, :, :], lp[:, :, 0, :], lp[:, :, 1, :], ALU.mult))
                nc.vector.reduce_sum(lams[:, 0:2], lamt[:, :, :], AX.X).then_inc(lam_sum, 1)
                ts(prm_("cw", 0, 32), prm_("cw", 0, 32), 0.5, None, ALU.mult)
                ts(prm_("fw", 0, 3 * FT), prm_("fw", 0, 3 * FT), 0.5, None, ALU.mult)
                ts(prm_("fb", 0, FT), prm_("fb", 0, FT), 0.5, None, ALU.mult)
                ts(bgh[:, :], prm_("bgate", 0, 24), 0.5, None, ALU.mult)
                step.then(tt(sg[:, :], prm_("subg"), prm_("oml"), ALU.mult))
                dve.wait_ge(wd_hi, l + 1)
                tt(wdl[:, :], prm_("wdt", 0, KT * 16), wdh[:, :].bitcast(F32), ALU.subtract)
                dve.wait_ge(lam_exp, l + 1)
                stt(out=nlam[:, :], in0=lams[:, 3:4], scalar=lams[:, 2:3], in1=prm_("li"), op0=ALU.subtract,
                    op1=ALU.subtract).then_inc(par_ready, 1)
                dve.wait_ge(par_ready, l + 1)

            def taps(l, g):
                kind, j = GROUPS[g]
                n = j if kind == XBC else 8 + j
                w = "cw" if kind == XBC else "fw"
                tile = j if kind == XBC else (j // 2 + FT * (j % 2))
                b = cv[:, j % 2, :]
                bank = acc[g % BANKS]
                dve.wait_ge(cv_init, count(l, NCONV, n))
                step.then(stt(out=b[:, 1:T], in0=bank[:, 0:T - 1], scalar=prm_(w, 3 * tile), in1=b[:, 1:T],
                              op0=ALU.mult, op1=ALU.add))
                stt(out=b[:, 0:T - 1], in0=bank[:, 1:T], scalar=prm_(w, 3 * tile + 2), in1=b[:, 0:T - 1],
                    op0=ALU.mult, op1=ALU.add).then_inc(cv_done, 1)

            def conv_result(l, g):
                kind, j = GROUPS[g]
                if kind == XBC:
                    dve.wait_ge(cv_tanh, count(l, 8 + FT, j))
                    stt(out=xbc[:, j, :], in0=th[:, j % 2, :], scalar=1.0, in1=cv[:, j % 2, :], op0=ALU.add,
                        op1=ALU.mult).then_inc(cv_out, 1)
                elif j % 2 == 0:
                    dve.wait_ge(cv_tanh, count(l, 8 + FT, 8 + j // 2))
                    stt(out=th[:, 0, :], in0=th[:, 0, :], scalar=1.0, in1=cv[:, 0, :], op0=ALU.add,
                        op1=ALU.mult).then_inc(cv_out, 1)
                else:
                    dve.wait_ge(cv_out, count(l, 8 + FT, 8 + j // 2))
                    dve.wait_ge(cv_done, count(l, NCONV, 8 + j))
                    tt(cv[:, 1, :], th[:, 0, :], cv[:, 1, :], ALU.mult).then_inc(h_full, 1)

            def rotate(l, kind, j):
                b = gates[:, 14 + (kind == KK), 0:LAT]
                dst = qt[:, j, 0:LAT] if kind == QQ else kt_[:, j, PAST:PAST + LAT]
                dve.wait_ge(qk_in, count(l, 2 * HEADS, j + HEADS * (kind == KK)))
                swap = [(k + 16) % 32 for k in range(32)]
                step.then(nc.vector.stream_shuffle(b, dst, swap))
                tt(dst, dst, cos, ALU.mult)
                step.then(tt(b, b, sin, ALU.mult))
                tt(dst, dst, b, ALU.add).then_inc(qk_done, 1)

            def branch(l, g):
                kind, j = GROUPS[g]
                b, jj = divmod(j, KT)
                group_done(dve, l, g)
                if j == 0:
                    dve.wait_ge(g_done, count(l, 24, 23))
                stt(out=gates[:, j, :], in0=gates[:, j, :], scalar=1.0, in1=acc[g % BANKS][:, 0:T],
                    op0=ALU.add, op1=ALU.mult).then_inc(gb_done, 1)
                if b == 2:
                    dve.wait_ge(gb_done, count(l, 24, j))
                    dve.wait_ge(mg_done, count(l, KT, jj))
                    if jj >= 2:
                        dve.wait_ge(h_hi, count(l, NSPLIT, SP_MG + jj - 2))
                    tt(cv[:, j % 2, :], gates[:, jj, :], gates[:, j, :], ALU.add).then_inc(h_full, 1)
                    low_merged.append(jj)

            def update(l, g):
                kind, j = GROUPS[g]
                group_done(dve, l, g)
                for v, (a0, a1) in enumerate(SEGS):
                    gate = g1h[:, j, v:v + 1] if kind == OUT else mod[:, 5 * KT + j, v:v + 1]
                    last = stt(out=x[:, j, a0:a1], in0=acc[g % BANKS][:, a0:a1], scalar=gate, in1=x[:, j, a0:a1],
                               op0=ALU.mult, op1=ALU.add)
                last.then_inc(x_new, 1)

            def softmax_max(l, i):
                nk = PAST + LAT if i % NCH < 2 else SEQ
                dve.wait_ge(s_done, count(l, NATT, i))
                nc.vector.reduce_max(mxb[:, i % 2, 0:1], mix5[:, 0:nk], AX.X)
                step.then(nc.vector.reduce_max(mxb[:, i % 2, 1:2], mix6[:, 0:nk], AX.X))
                if i >= 2:
                    dve.wait_ge(exp_done, count(l, NATT, i - 2))
                ts(nmb[:, i % 2, :], mxb[:, i % 2, :], -SCALE, None, ALU.mult).then_inc(nm_done, 1)

            def softmax_mix(l, i):
                nk = PAST + LAT if i % NCH < 2 else SEQ
                dve.wait_ge(exp_done, count(l, NATT, i))
                step.then(nc.vector.reciprocal(rcp[:, 0:2], rsm[:, i % 2, :]))
                step.then(tt(rcp[:, 2:3], rcp[:, 1:2], nlam[:, :], ALU.mult))
                p0, p1 = pr[:, i % 2, 0, 0:nk], pr[:, i % 2, 1, 0:nk]
                step.then(ts(p1, p1, rcp[:, 2:3], None, ALU.mult))
                stt(out=p0, in0=p0, scalar=rcp[:, 0:1], in1=p1, op0=ALU.mult, op1=ALU.add).then_inc(a_done, 1)

            def weighted(l, k):
                c, d = S_TASKS[k]
                if k:
                    dve.wait_ge(cst_done, count(l, 4, k - 1))
                n = NCH * SSD_H
                w_ = wdc[:, n * d + SSD_H * c:n * d + SSD_H * c + SSD_H]
                tt(xw[:, :].rearrange("p (h q) -> p h q", h=SSD_H), xt[:, c, :].rearrange("p (h q) -> p h q", h=SSD_H),
                   w_.unsqueeze(2).to_broadcast([P, SSD_H, SSD_P]), ALU.mult).then_inc(xw_done, 1)

            def enter_state(l, k):
                c, d = S_TASKS[k]
                dve.wait_ge(cst_done, count(l, 4, k))
                dve.wait_ge(state_in, 32 * (l + 1))
                tot = ede[:, 48 + 16 * c + SSD_H * d:48 + 16 * c + SSD_H * d + SSD_H]
                step.then(tt(hst[:, 2 + k, :].rearrange("p (h q) -> p h q", h=SSD_H),
                             hst[:, d, :].rearrange("p (h q) -> p h q", h=SSD_H),
                             tot.unsqueeze(2).to_broadcast([P, SSD_H, SSD_P]), ALU.mult))
                tt(hst[:, 2 + k, :], hst[:, 2 + k, :], mix7[:, :], ALU.add).then_inc(st_done, 1)

            def decays(l, y_):
                c, g = divmod(y_, 2)
                dve.wait_ge(bc_done, count(l, NY, y_))
                if y_:
                    dve.wait_ge(y_done, count(l, NY, y_ - 1))
                else:
                    dve.wait_ge(on_done, l + 1)
                n = NCH * SSD_H
                for d, bank in enumerate((mix5, mix6)):
                    for i in range(4):
                        col = n * d + SSD_H * c + 4 * g + i
                        last = stt(out=ee[:, d, P * i:P * i + P], in0=bank[:, P * i:P * i + P], scalar=nac[:, col:col + 1],
                                   in1=neg[d], op0=ALU.add, op1=ALU.add)
                last.then_inc(d_done, 1)

            def matrices(l, y_):
                c, g = divmod(y_, 2)
                dve.wait_ge(e_done, count(l, NY, y_))
                for d in range(2):
                    for i in range(4):
                        col = 16 * c + SSD_H * d + 4 * g + i
                        m_ = ee[:, d, P * i:P * i + P]
                        last = stt(out=m_, in0=m_, scalar=dtt[:, col:col + 1], in1=bg[:, c, P * (2 + g):P * (3 + g)],
                                   op0=ALU.mult, op1=ALU.mult)
                    if c < 2:
                        e3 = eb[:, d, :].rearrange("p (i t) -> p i t", i=4)
                        last = tt(e3, e3, xbc[:, 6 + g, CHUNK0[c]:CHUNK0[c] + P].unsqueeze(1).to_broadcast([P, 4, P]),
                                  ALU.mult)
                last.then_inc(m_done, 1)

            def gate_z(l, y_):
                c, g = divmod(y_, 2)
                tok = slice(CHUNK0[c], CHUNK0[c] + P)
                dve.wait_ge(y_done, count(l, NY, y_))
                if y_ == 0:
                    dve.wait_ge(st_out, 32 * (l + 1))
                for i in range(2):
                    t_ = 2 * g + i
                    step.then(stt(out=cv[:, 0, P * i:P * i + P], in0=xbc[:, t_, tok], scalar=prm_("ssdD", t_),
                                  in1=mix7[:, P * i:P * i + P], op0=ALU.mult, op1=ALU.add))
                for i in range(2):
                    t_ = 2 * g + i
                    last = stt(out=zz[:, t_, tok], in0=cv[:, 0, P * i:P * i + P], scalar=0.5, in1=zz[:, t_, tok],
                               op0=ALU.mult, op1=ALU.mult)
                last.then_inc(yz_done, 1)

            def mixers_a(l, s):
                if s < NATT:
                    softmax_max(l, s)
                if s == 1:
                    dve.wait_ge(misc_done, count(l, NMISC, M_DTT))
                    step.then(tt(dtv[:, :].rearrange("p (c h) -> p c h", c=NCH),
                                 mz[:, 0:48].rearrange("p (c h) -> p c h", c=NCH),
                                 prm_("dtb", 0, 16).unsqueeze(1).to_broadcast([P, NCH, 16]), ALU.add))
                    stt(out=dte[:, :], in0=dtv[:, :], scalar=-1.0, in1=dtv[:, :], op0=ALU.mult, op1=ALU.min) \
                        .then_inc(dt_raw, 1)
                if s == 2:
                    dve.wait_ge(dt_log, l + 1)
                    step.then(stt(out=dtt[:, :], in0=dtv[:, :], scalar=0.0, in1=dte[:, :], op0=ALU.max, op1=ALU.add))
                    stt(out=adt[:, :].rearrange("p (c h) -> p c h", c=NCH), in0=dtt[:, :].rearrange("p (c h) -> p c h", c=NCH),
                        scalar=-1.0, in1=eal[:, :].unsqueeze(1).to_broadcast([P, NCH, 16]), op0=ALU.mult,
                        op1=ALU.mult).then_inc(adt_done, 1)
                if s == 3:
                    dve.wait_ge(misc_done, count(l, NMISC, M_SM))
                    nc.vector.tensor_copy(sm[:, :], mz[:, 0:144]).then_inc(sm_done, 1)
                    dve.wait_ge(sm_done, l + 1)
                    ts(nac[:, :], sm[:, 0:48], -1.0, None, ALU.mult)
                    dve.wait_ge(ede_done, l + 1)
                    for d in range(2):
                        last = tt(wdc[:, 24 * d:24 * d + 24].rearrange("p (c h) -> p c h", c=NCH),
                                  dtt[:, :].rearrange("p (c h) -> p c h", c=NCH)[:, :, SSD_H * d:SSD_H * d + SSD_H],
                                  ede[:, 24 * d:24 * d + 24].rearrange("p (c h) -> p c h", c=NCH), ALU.mult)
                    last.then_inc(wdc_done, 1)
                if SLOT_PW <= s < SLOT_PW + 4:
                    j = s - SLOT_PW
                    dve.wait_ge(misc_done, count(l, NMISC, M_PW + j))
                    ts(ut[:, j, 0:T], mz, prm_("pscale", j), None, ALU.mult).then_inc(op_done, 1)
                if s == SLOT_SPLIT:
                    for i in range(4):
                        low(l, SP_OP + i, hl[:, i, :], ut[:, i, 0:T], hh[:, i, :])
                if scan_task(s, Y_SLOTS) is not None:
                    gate_z(l, scan_task(s, Y_SLOTS))
                if scan_task(s) is not None:
                    decays(l, scan_task(s))

            def mixers_b(l, s):
                if s < NATT:
                    softmax_mix(l, s)
                if s in ROTATE_SLOTS:
                    i = ROTATE_SLOTS.index(s)
                    rotate(l, (QQ, KK)[i % 2], i // 2 + 1)
                if SLOT_S <= s < SLOT_S + 2:
                    enter_state(l, s - SLOT_S)
                if SLOT_S - 1 <= s < SLOT_S + 3:
                    if s == SLOT_S - 1:
                        dve.wait_ge(xt_in, count(l, NCH, NCH - 1))
                        dve.wait_ge(wdc_done, l + 1)
                    weighted(l, s - SLOT_S + 1)
                if s == SLOT_X + HEADS:
                    dve.wait_ge(ors_done, l + 1)
                    for h in range(HEADS):
                        last = stt(out=ot[:, h, :], in0=ot[:, h, :], scalar=sg[:, 0:1], in1=rst[:, h, :], op0=ALU.mult,
                                   op1=ALU.mult)
                    last.then_inc(on_done, 1)
                if scan_task(s) is not None:
                    matrices(l, scan_task(s))
                if s == SLOT_SPLIT + 1:
                    for i in range(4):
                        low(l, SP_OT + i, hl[:, 4 + i, :], ot[:, i, :], hh[:, 4 + i, :])
                if s == SLOT_RMS + 1:
                    dve.wait_ge(zrs_done, l + 1)
                    for i in range(4):
                        stt(out=zz[:, i, :], in0=zz[:, i, :], scalar=prm_("ssdg", i), in1=rst[:, 2 * (i // 2), :],
                            op0=ALU.mult, op1=ALU.mult).then_inc(zn_done, 1)
                    for i in range(4):
                        low(l, SP_Z + i, osl[:, i, :], zz[:, i, :], osh[:, i, :])

            low_merged = []
            dve.wait_ge(cs_in, 32)
            ts(csh[:, :], cs[:, :], 0.5, None, ALU.mult).then_inc(cs_half, 1)
            dve.wait_ge(cs_tanh, 1)
            stt(out=cs[:, :], in0=cst[:, :], scalar=1.0, in1=csh[:, :], op0=ALU.add, op1=ALU.mult).then_inc(cs_ready, 1)
            dve.wait_ge(zeroed, 2)
            for l in range(DEPTH):
                if l == 0:
                    rows_silu(0)
                    head_half(0)
                    for u in range(AHEAD):
                        lo(l, u)
                    norm(l, 0, SP_N1, lambda: head_half(1))
                    dve.wait_ge(tab_in, 16)
                    params(l)
                else:
                    norm(l, 0, SP_N1)
                for u in range(NU):
                    if u == UP0:
                        norm(l, 1, SP_N2)
                        rows_silu(l + 1)
                    if u == PREP and l + 1 < DEPTH:
                        params(l + 1)
                        summed(l + 1, 0, MOD_HEAD)
                        scale_of(sc1, norm1_weight(l + 1), KT).then_inc(scale_ready, 1)
                    if u in (0, UP0):
                        ahead(l, u)
                    done = done_after(u)
                    for g in done:
                        if GROUPS[g][0] in (XBC, UP):
                            group_done(dve, l, g)
                            taps(l, g)
                        if GROUPS[g][0] == BRANCH:
                            branch(l, g)
                    if MIX0 <= u <= MIX0 + SLOT_RMS + 1:
                        mixers_a(l, u - MIX0)
                    last_update = UNITS[u] in ((OUT, KT - 1, 0), (DOWN, KT - 1, 2))
                    if u not in (0, UP0) and not last_update:
                        ahead(l, u)
                    for g in done:
                        kind, j = GROUPS[g]
                        if kind in (XBC, UP):
                            conv_result(l, g)
                            if kind == UP and j % 2:
                                low(l, SP_FF + j // 2, al[:, j // 2, :], cv[:, 1, :], ah[:, j // 2, :])
                        if kind in (QQ, KK) and j == 0:
                            rotate(l, kind, 0)
                        if kind == ZZ:
                            dve.wait_ge(z_tanh, count(l, 4, j))
                            stt(out=zz[:, j, :], in0=th[:, j % 2, :], scalar=1.0, in1=acc[g % BANKS][:, 0:T],
                                op0=ALU.add, op1=ALU.mult).then_inc(z_done, 1)
                        if kind in (OUT, DOWN):
                            update(l, g)
                    while low_merged:
                        jj = low_merged.pop(0)
                        low(l, SP_MG + jj, ml[:, jj, :], cv[:, jj % 2, :], mh[:, jj, :])
                    if MIX0 <= u <= MIX0 + SLOT_RMS + 1:
                        mixers_b(l, u - MIX0)
                    if last_update:
                        ahead(l, u)
                    modulation(l, u)
                    if u == MOD_G2 - MOD_HEAD - 1:
                        summed(l, MOD_HEAD, MOD_G2)
                        scale_of(sc2, prm_("n2g", 0, KT), 4 * KT).then_inc(scale_ready, 1)
                        step.then(ts(g1h[:, :, :], mod[:, 2 * KT:3 * KT, :], 0.5, None, ALU.mult))
                    if u == G2_LAST:
                        summed(l, MOD_G2, MODT)
            dve.wait_ge(fg_in, 16)
            dve.wait_ge(rs_ready, 2 * DEPTH + 1)
            for j in range(KT):
                stt(out=gates[:, j, :], in0=x[:, j, :], scalar=fg[:, j:j + 1], in1=rs[:, :], op0=ALU.mult,
                    op1=ALU.mult).then_inc(y_ready, 1)


def _tiles(a):
    return a.reshape(-1, P, a.shape[-1]).transpose(1, 0, 2)


def _stream(w_in, w_gate, w_branch, w_out, w_up, w_down, w_mod):
    c0 = {UU: 0, QQ: 512, KK: 1024, VV: 1536, ZZ: 2048, XBC: 2560}
    w_in, w_gate, w_branch, w_out, w_up, w_down = (_tiles(w) for w in (w_in, w_gate, w_branch, w_out, w_up, w_down))
    out = {}
    for what, n in [("mod", m) for m in range(MODT)] + [("w", u) for u in range(NU)]:
        if what == "mod":
            a = w_mod[:, P * n:P * n + P].T
        else:
            kind, j, part = UNITS[n]
            col = slice(P * j, P * j + P)
            if kind == VV:
                a = w_in[:, 2 * part:2 * part + 2, c0[VV]:c0[VV] + 4 * P]
            elif kind in c0:
                a = w_in[:, :, c0[kind] + P * j:c0[kind] + P * j + P]
            elif kind == GATE:
                a = w_gate[:, :, col]
            elif kind == BRANCH:
                b, jj = divmod(j, KT)
                rows = w_branch[:, 4 * b:4 * b + 4, :]
                a = np.concatenate([rows[:, :, P * t:P * t + P] for t in (jj, jj + 1)], axis=1)
            elif kind == OUT:
                a = w_out[:, :, col]
            elif kind == UP:
                t = j // 2 + FT * (j % 2)
                a = w_up[:, :, P * t:P * t + P]
            else:
                a = w_down[:, DOWN_CUTS[part][0]:DOWN_CUTS[part][1], col]
        out[what, n] = a.reshape(P, -1)
    return out


def kernel(**inputs):
    import concourse.bacc as _bacc
    from concourse.bass_utils import run_bass_kernel_spmd as _run

    v = {k: np.ascontiguousarray(a) for k, a in inputs.items()}

    def per_channel(a):
        return a.reshape(-1, P).T

    def everywhere(a):
        return np.broadcast_to(a.reshape(1, -1), (P, a.size))

    par = np.zeros((DEPTH, P, NPAR), np.float32)
    for l in range(DEPTH):
        lam_init = 0.8 - 0.6 * float(np.exp(-0.3 * l))
        taps = {n: v[k][l].reshape(3, -1, P).transpose(2, 1, 0).reshape(P, -1)
                for n, k in (("cw", "ssd_conv_w"), ("fw", "ffn_conv_w"))}
        cols = {
            "n2g": per_channel(v["norm2_g"][l]),
            "pscale": per_channel(v["pool_scale"][l]), "subg": per_channel(v["att_subln_g"][l]),
            "li": np.full((P, 1), lam_init), "oml": np.full((P, 1), 1.0 - lam_init),
            "cw": taps["cw"], "cb": per_channel(v["ssd_conv_b"][l]), "ssdg": per_channel(v["ssd_norm_g"][l]),
            "ssdD": per_channel(np.repeat(v["ssd_D"][l], SSD_P)), "bgate": per_channel(v["b_gate"][l]),
            "fw": taps["fw"], "fb": per_channel(v["ffn_conv_b"][l]), "dtb": everywhere(v["ssd_dt_bias"][l]),
            "alog": everywhere(v["ssd_A_log"][l]), "lam": everywhere(v["att_lambda"][l]),
            "wdt": _tiles(v["w_in"][l][:, 3584:3600]).reshape(P, -1),
            "plw": v["pool_w"][l].transpose(1, 0, 2).reshape(P, -1),
        }
        for name, a in cols.items():
            at, n = PAR[name]
            par[l, :, at:at + n] = a

    def token_tiles(a):
        return a.T.reshape(KT, P, -1).transpose(1, 0, 2)

    units = [_stream(*(v[k][l] for k in ("w_in", "w_gate", "w_branch", "w_out", "ffn_w_up", "ffn_w_down", "w_mod")))
             for l in range(DEPTH)]
    head_tiles = _tiles(v["w_mod"][0])
    wstream = np.zeros((NS, P, KT * P), np.float32)
    for i, (l, what, u) in enumerate(STREAM):
        lw, n = mod_after(l, u) if what == "mod" else (l, u)
        a = units[lw][what, n]
        wstream[i, :, :a.shape[1]] = a

    kcache = v["cache_attn_k"][0]
    ins = {
        "wstream": wstream,
        "whead": np.stack([np.concatenate([head_tiles[:, :, P * j:P * j + P].reshape(P, -1), units[0]["mod", KT + j]], axis=1)
                           for j in range(KT)]),
        "par": par,
        "bias": np.concatenate([per_channel(v["b_mod"]), per_channel(v["norm1_g"])], axis=1),
        "tab": tables(),
        "xs": token_tiles(v["x_sample"][0]),
        "xp": token_tiles(v["x_prompt"][0]),
        "cvec": np.stack([per_channel(v["c"][0]), per_channel(v["c_ctx"])], axis=2).reshape(P, 2 * KT),
        "cvec_rows": np.broadcast_to(np.stack([v["c"][0], v["c_ctx"]]), (P, 2, D)),
        "kc": kcache.transpose(0, 3, 4, 2, 1).reshape(DEPTH, P, HEADS, PAST),
        "vc": v["cache_attn_v"][0].reshape(DEPTH, PAST, 4 * P),
        "st0": v["state_ssd"][0].transpose(0, 1, 4, 2, 3).reshape(DEPTH, 2, P, 4 * P),
        "fng": per_channel(v["final_norm_g"]),
    }
    outs = {"y": (P, KT, T), "newk": (DEPTH, P, HEADS, SEQ), "newv": (DEPTH, P, 4 * P), "news": (DEPTH, 2, P, 4 * P)}
    nc = _bacc.Bacc("TRN2", target_bir_lowering=False, num_devices=1)
    arrays, args = {}, []
    for name, a in ins.items():
        a = np.ascontiguousarray(a, dtype=np.float32)
        arrays[f"in_{name}_dram"] = a
        args.append(nc.dram_tensor(f"in_{name}_dram", a.shape, F32, kind="ExternalInput").ap())
    for name, shape in outs.items():
        args.append(nc.dram_tensor(f"out_{name}_dram", shape, F32, kind="ExternalOutput").ap())
    build(nc, *args)
    res = _run(nc, [arrays], core_ids=[0]).results[0]
    yt = res["out_y_dram"].transpose(2, 1, 0).reshape(T, D)
    nk = res["out_newk_dram"].reshape(DEPTH, 2, QK, HEADS, SEQ).transpose(0, 4, 3, 1, 2)
    nv = res["out_newv_dram"].reshape(DEPTH, SEQ, HEADS, 2 * QK)
    ns = res["out_news_dram"].reshape(DEPTH, 2, P, SSD_H, SSD_P).transpose(0, 1, 3, 4, 2)
    return tuple(np.ascontiguousarray(a[None]) for a in (yt[CTX0:], yt[:LAT], nk, nv, ns))
```
